# Optimizing a Trainium2 kernel written in Bass

```python
import jax, jax.numpy as jnp
from jax import lax
import numpy as np

D_MODEL = 1024
BATCH = 1
SEQ = 256
DEPTH = 2

HEAD_DIM = 64
A_HEADS = 8
A_KV_HEADS = 2
A_WIDTH = A_HEADS * HEAD_DIM
A_KV_WIDTH = A_KV_HEADS * HEAD_DIM
IDX_HEADS = 4
IDX_DIM = 64
IDX_SCALE = (IDX_HEADS * IDX_DIM) ** -0.5
TOPK_MAX = 256
POOL_WINDOWS = (2, 4, 8, 16)
POOL_GROUP = 128
POOL_WIDTH = POOL_GROUP * len(POOL_WINDOWS)
EVEN_MIX_WIDTH = A_WIDTH + POOL_WIDTH
EVEN_IN_COLS = A_WIDTH + 2 * A_KV_WIDTH + IDX_HEADS * IDX_DIM + IDX_DIM + IDX_HEADS + POOL_WIDTH
C_HEADS = 16
C_WIDTH = C_HEADS * HEAD_DIM
D_FF = -(-8 * D_MODEL // (3 * 256)) * 256
N_EVEN = (DEPTH + 1) // 2
N_ODD = DEPTH // 2
Q_BLOCK = 128
EPS = 1e-6


def rms_norm(x, g):
    x32 = x.astype(jnp.float32)
    y = x32 * lax.rsqrt(jnp.mean(x32 * x32, axis=-1, keepdims=True) + EPS)
    return (y * g.astype(jnp.float32)).astype(x.dtype)

def to_blocks(a):
    b, t = a.shape[:2]
    a = a.reshape((b, t // Q_BLOCK, Q_BLOCK) + a.shape[2:])
    return jnp.moveaxis(a, 1, 0)

def from_blocks(a):
    a = jnp.moveaxis(a, 0, 1)
    return a.reshape((a.shape[0], a.shape[1] * a.shape[2]) + a.shape[3:])

def dsa_attention(q, k, v, q_idx, k_idx, w_idx):
    b, t = q.shape[:2]
    n_sel = min(TOPK_MAX, t // 4)
    rep = A_HEADS // A_KV_HEADS
    key_pos = jnp.arange(t)
    gather = jax.vmap(lambda kv, ids: kv[ids])

    def block(args):
        qb, qib, wb, start = args
        q_pos = start + jnp.arange(Q_BLOCK)
        causal = key_pos[None, :] <= q_pos[:, None]
        rel = jax.nn.relu(jnp.einsum('bthd,bsd->bths', qib, k_idx).astype(jnp.float32))
        score = jnp.einsum('bths,bth->bts', rel, wb.astype(jnp.float32)) * IDX_SCALE
        score = jnp.where(causal[None], score, -jnp.inf)
        _, sel = lax.top_k(score, n_sel)
        k_sel = gather(k, sel)
        v_sel = gather(v, sel)
        valid = sel <= q_pos[None, :, None]
        qg = qb.reshape(b, Q_BLOCK, A_KV_HEADS, rep, HEAD_DIM)
        logits = jnp.einsum('btgrd,btkgd->btgrk', qg, k_sel).astype(jnp.float32) * (HEAD_DIM ** -0.5)
        logits = jnp.where(valid[:, :, None, None, :], logits, -jnp.inf)
        p = jax.nn.softmax(logits, axis=-1).astype(v.dtype)
        o = jnp.einsum('btgrk,btkgd->btgrd', p, v_sel)
        return o.reshape(b, Q_BLOCK, A_WIDTH)

    starts = jnp.arange(t // Q_BLOCK) * Q_BLOCK
    out = lax.map(block, (to_blocks(q), to_blocks(q_idx), to_blocks(w_idx), starts))
    return from_blocks(out)

def multiscale_pool(u, pool_w, pool_scale):
    b, t, _ = u.shape
    groups = u.astype(jnp.float32).reshape(b, t, len(POOL_WINDOWS), POOL_GROUP)
    c0 = jnp.pad(jnp.cumsum(groups, axis=1), ((0, 0), (1, 0), (0, 0), (0, 0)))
    pos = jnp.arange(1, t + 1, dtype=jnp.float32)
    outs = []
    for g, w in enumerate(POOL_WINDOWS):
        cg = c0[:, :, g]
        hi = cg[:, 1:]
        lo = jnp.pad(cg[:, :t + 1 - w], ((0, 0), (w - 1, 0), (0, 0)))
        count = jnp.minimum(pos, float(w))[None, :, None]
        outs.append((hi - lo) / count - groups[:, :, g])
    mixed = jnp.stack(outs, axis=2)
    y = jnp.einsum('btgc,gcd->btgd', mixed, pool_w.astype(jnp.float32))
    return (y.reshape(b, t, POOL_WIDTH) * pool_scale.astype(jnp.float32)).astype(u.dtype)

def stick_breaking_attention(q, k, v):
    b, t = q.shape[:2]
    key_pos = jnp.arange(t)

    def block(args):
        qb, start = args
        q_pos = start + jnp.arange(Q_BLOCK)
        strict = key_pos[None, :] < q_pos[:, None]
        z = jnp.einsum('bthd,bshd->bhts', qb, k).astype(jnp.float32) * (HEAD_DIM ** -0.5)
        brk = jnp.where(strict, jax.nn.softplus(z), 0.0)
        later = jnp.pad(brk[..., 1:], ((0, 0), (0, 0), (0, 0), (0, 1)))
        remain = lax.cumsum(later, axis=3, reverse=True)
        log_a = jax.nn.log_sigmoid(z) - remain
        a = jnp.where(strict, jnp.exp(log_a), 0.0).astype(v.dtype)
        o = jnp.einsum('bhts,bshd->bthd', a, v)
        return o.reshape(b, Q_BLOCK, C_WIDTH)

    starts = jnp.arange(t // Q_BLOCK) * Q_BLOCK
    out = lax.map(block, (to_blocks(q), starts))
    return from_blocks(out)

def even_mixer(h, w_in, w_out, q_g, k_g, pool_w, pool_scale):
    b, t, _ = h.shape
    proj = h @ w_in
    sizes = [A_WIDTH, A_KV_WIDTH, A_KV_WIDTH, IDX_HEADS * IDX_DIM, IDX_DIM, IDX_HEADS]
    offsets = np.cumsum(sizes).tolist()
    q, k, v, qi, ki, wi, u = jnp.split(proj, offsets, axis=-1)
    q = rms_norm(q.reshape(b, t, A_HEADS, HEAD_DIM), q_g)
    k = rms_norm(k.reshape(b, t, A_KV_HEADS, HEAD_DIM), k_g)
    v = v.reshape(b, t, A_KV_HEADS, HEAD_DIM)
    attn = dsa_attention(q, k, v, qi.reshape(b, t, IDX_HEADS, IDX_DIM), ki, wi)
    pooled = multiscale_pool(u, pool_w, pool_scale)
    return jnp.concatenate([attn, pooled], axis=-1) @ w_out

def odd_mixer(h, w_qkv, w_out):
    b, t, _ = h.shape
    q, k, v = jnp.split((h @ w_qkv).reshape(b, t, 3, C_HEADS, HEAD_DIM), 3, axis=2)
    o = stick_breaking_attention(q[:, :, 0], k[:, :, 0], v[:, :, 0])
    return o @ w_out

def swiglu(h, w1, w3, w2):
    return (jax.nn.silu(h @ w1) * (h @ w3)) @ w2

def first_inputs(seed: int = 0) -> dict:
    key = jax.random.key(seed)
    ks = jax.random.split(key, 16)
    f32 = jnp.float32

    def dense(k, shape):
        return jax.random.normal(k, shape, f32) * (shape[-2] ** -0.5)

    def gain(k, shape, s):
        return 1.0 + s * jax.random.normal(k, shape, f32)

    return {
        'x': jax.random.normal(ks[0], (BATCH, SEQ, D_MODEL), f32),
        'norm_mix_g': gain(ks[1], (DEPTH, D_MODEL), 0.05),
        'norm_ffn_g': gain(ks[2], (DEPTH, D_MODEL), 0.05),
        'ev_w_in': dense(ks[3], (N_EVEN, D_MODEL, EVEN_IN_COLS)),
        'ev_w_out': dense(ks[4], (N_EVEN, EVEN_MIX_WIDTH, D_MODEL)),
        'ev_q_norm_g': gain(ks[5], (N_EVEN, HEAD_DIM), 0.05),
        'ev_k_norm_g': gain(ks[6], (N_EVEN, HEAD_DIM), 0.05),
        'ev_pool_w': dense(ks[7], (N_EVEN, len(POOL_WINDOWS), POOL_GROUP, POOL_GROUP)),
        'ev_pool_scale': gain(ks[8], (N_EVEN, POOL_WIDTH), 0.1),
        'od_w_qkv': dense(ks[9], (N_ODD, D_MODEL, 3 * C_WIDTH)),
        'od_w_out': dense(ks[10], (N_ODD, C_WIDTH, D_MODEL)),
        'ffn_w1': dense(ks[11], (DEPTH, D_MODEL, D_FF)),
        'ffn_w3': dense(ks[12], (DEPTH, D_MODEL, D_FF)),
        'ffn_w2': dense(ks[13], (DEPTH, D_FF, D_MODEL)),
    }

def first_block(x, norm_mix_g, norm_ffn_g, ev_w_in, ev_w_out, ev_q_norm_g, ev_k_norm_g,
              ev_pool_w, ev_pool_scale, od_w_qkv, od_w_out, ffn_w1, ffn_w3, ffn_w2):
    for layer in range(DEPTH):
        i = layer // 2
        h = rms_norm(x, norm_mix_g[layer])
        if layer % 2 == 0:
            x = x + even_mixer(h, ev_w_in[i], ev_w_out[i], ev_q_norm_g[i], ev_k_norm_g[i],
                               ev_pool_w[i], ev_pool_scale[i])
        else:
            x = x + odd_mixer(h, od_w_qkv[i], od_w_out[i])
        h = rms_norm(x, norm_ffn_g[layer])
        x = x + swiglu(h, ffn_w1[layer], ffn_w3[layer], ffn_w2[layer])
    return x


DEPTH_2 = 1

RET_HEADS = 4
RET_DK = 128
RET_DV = 256
RET_CHUNK = 128
ROPE_BASE = 10000.0
MOBA_HEADS = 8
MOBA_DH = 64
MOBA_BLOCK = 256
MOBA_TOPK = 3
MOBA_QBLOCK = 64
FFN_HIDDEN = ((8 * D_MODEL + 3 * 256 - 1) // (3 * 256)) * 256

RET_QK = RET_HEADS * RET_DK
RET_V = RET_HEADS * RET_DV
MOBA_W = MOBA_HEADS * MOBA_DH
IN_SPLITS = (RET_QK, RET_QK, RET_V, RET_V, MOBA_W, MOBA_W, MOBA_W, D_MODEL, D_MODEL)
IN_COLS = sum(IN_SPLITS)

RMS_EPS = 1e-6
GN_EPS = 1e-5
NEG = -1e30


def rmsnorm(x, w):
    xf = x.astype(jnp.float32)
    y = xf * lax.rsqrt(jnp.mean(xf * xf, axis=-1, keepdims=True) + RMS_EPS)
    return (y * w.astype(jnp.float32)).astype(x.dtype)

def rotary(x, pos):
    half = x.shape[-1] // 2
    inv = ROPE_BASE ** (-jnp.arange(half, dtype=jnp.float32) / half)
    ang = pos.astype(jnp.float32)[:, None] * inv[None, :]
    cos = jnp.cos(ang)[None, :, None, :].astype(x.dtype)
    sin = jnp.sin(ang)[None, :, None, :].astype(x.dtype)
    x1, x2 = x[..., :half], x[..., half:]
    return jnp.concatenate([x1 * cos - x2 * sin, x2 * cos + x1 * sin], axis=-1)

def retention(q, k, v):
    B, S, H, _ = q.shape
    dv = v.shape[-1]
    C = RET_CHUNK
    NC = S // C
    dt = q.dtype

    def chunks(t):
        return t.reshape(B, NC, C, H, t.shape[-1]).transpose(0, 3, 1, 2, 4)

    qc, kc, vc = chunks(q), chunks(k), chunks(v)
    lg = jnp.log1p(-jnp.exp2(-5.0 - jnp.arange(H, dtype=jnp.float32)))
    idx = jnp.arange(C, dtype=jnp.float32)
    diff = idx[:, None] - idx[None, :]
    dmat = jnp.where(diff >= 0, jnp.exp(jnp.maximum(diff, 0.0)[None] * lg[:, None, None]), 0.0).astype(dt)
    xi = jnp.exp((idx + 1.0)[None, :] * lg[:, None]).astype(dt)
    zeta = jnp.exp((C - 1.0 - idx)[None, :] * lg[:, None]).astype(dt)
    g_chunk = jnp.exp(C * lg).astype(dt)

    scores = jnp.einsum('bhcnd,bhcmd->bhcnm', qc, kc) * dmat[None, :, None]
    o_inner = jnp.einsum('bhcnm,bhcme->bhcne', scores, vc)
    upd = jnp.einsum('bhcmd,bhcme->bhcde', kc * zeta[None, :, None, :, None], vc)
    upd = jnp.moveaxis(upd, 2, 0)

    def step(state, u):
        return g_chunk[None, :, None, None] * state + u, state

    _, r_prev = lax.scan(step, jnp.zeros_like(upd[0]), upd)
    r_prev = jnp.moveaxis(r_prev, 0, 2)
    o_cross = jnp.einsum('bhcnd,bhcde->bhcne', qc * xi[None, :, None, :, None], r_prev)
    o = (o_inner + o_cross).transpose(0, 2, 3, 1, 4).reshape(B, S, H, dv)
    of = o.astype(jnp.float32)
    mu = jnp.mean(of, axis=-1, keepdims=True)
    var = jnp.mean(jnp.square(of - mu), axis=-1, keepdims=True)
    o = ((of - mu) * lax.rsqrt(var + GN_EPS)).astype(dt)
    return o.reshape(B, S, H * dv)

def gather_blocks(blocks, sel):
    return jax.vmap(jax.vmap(lambda bl, ix: bl[ix]))(blocks, sel)

def moba_attention(q, k, v):
    B, S, H, dh = q.shape
    BLK, QB = MOBA_BLOCK, MOBA_QBLOCK
    sp = ((S + BLK - 1) // BLK) * BLK
    pad = ((0, 0), (0, sp - S), (0, 0), (0, 0))
    qh = jnp.pad(q, pad).transpose(0, 2, 1, 3)
    kh = jnp.pad(k, pad).transpose(0, 2, 1, 3)
    vh = jnp.pad(v, pad).transpose(0, 2, 1, 3)
    nb = sp // BLK
    kb = kh.reshape(B, H, nb, BLK, dh)
    vb = vh.reshape(B, H, nb, BLK, dh)
    kbar = jnp.mean(kb, axis=3)
    topk = min(MOBA_TOPK, nb)
    scale = dh ** -0.5
    n_qb = sp // QB

    def one_block(qi):
        start = qi * QB
        blk = start // BLK
        qb = lax.dynamic_slice_in_dim(qh, start, QB, axis=2)
        gate = jnp.einsum('bhqd,bhnd->bhqn', qb, kbar).astype(jnp.float32)
        gate = jnp.where(jnp.arange(nb)[None, None, None, :] < blk, gate, NEG)
        _, sel = lax.top_k(gate, topk)
        valid = sel < blk
        ks = gather_blocks(kb, sel)
        vs = gather_blocks(vb, sel)
        s_sel = jnp.einsum('bhqd,bhqkjd->bhqkj', qb, ks).astype(jnp.float32) * scale
        s_sel = jnp.where(valid[..., None], s_sel, NEG).reshape(B, H, QB, topk * BLK)
        k_own = lax.dynamic_index_in_dim(kb, blk, axis=2, keepdims=False)
        v_own = lax.dynamic_index_in_dim(vb, blk, axis=2, keepdims=False)
        s_own = jnp.einsum('bhqd,bhjd->bhqj', qb, k_own).astype(jnp.float32) * scale
        qpos = start + jnp.arange(QB)
        kpos = blk * BLK + jnp.arange(BLK)
        s_own = jnp.where(kpos[None, :] <= qpos[:, None], s_own, NEG)
        p = jax.nn.softmax(jnp.concatenate([s_sel, s_own], axis=-1), axis=-1)
        p_sel = p[..., :topk * BLK].reshape(B, H, QB, topk, BLK).astype(v.dtype)
        p_own = p[..., topk * BLK:].astype(v.dtype)
        return (jnp.einsum('bhqkj,bhqkjd->bhqd', p_sel, vs)
                + jnp.einsum('bhqj,bhjd->bhqd', p_own, v_own))

    out = lax.map(one_block, jnp.arange(n_qb))
    out = out.transpose(1, 0, 3, 2, 4).reshape(B, sp, H * dh)
    return out[:, :S]

def second_inputs(seed: int = 0) -> dict:
    key = jax.random.key(seed)
    ks = jax.random.split(key, 12)

    def w(k, shape, fan_in):
        return jax.random.normal(k, shape, jnp.float32) * fan_in ** -0.5

    def gain(k, shape):
        return 1.0 + 0.02 * jax.random.normal(k, shape, jnp.float32)

    return {
        "x": jax.random.normal(ks[0], (BATCH, SEQ, D_MODEL), jnp.float32),
        "norm1_w": gain(ks[1], (DEPTH_2, D_MODEL)),
        "w_in": w(ks[2], (DEPTH_2, D_MODEL, IN_COLS), D_MODEL),
        "q_norm_w": gain(ks[3], (DEPTH_2, MOBA_DH)),
        "k_norm_w": gain(ks[4], (DEPTH_2, MOBA_DH)),
        "w_ret_out": w(ks[5], (DEPTH_2, RET_V, D_MODEL), RET_V),
        "w_moba_out": w(ks[6], (DEPTH_2, MOBA_W, D_MODEL), MOBA_W),
        "w_o": w(ks[7], (DEPTH_2, D_MODEL, D_MODEL), D_MODEL),
        "norm2_w": gain(ks[8], (DEPTH_2, D_MODEL)),
        "w_ffn_gate": w(ks[9], (DEPTH_2, D_MODEL, FFN_HIDDEN), D_MODEL),
        "w_ffn_up": w(ks[10], (DEPTH_2, D_MODEL, FFN_HIDDEN), D_MODEL),
        "w_ffn_down": w(ks[11], (DEPTH_2, FFN_HIDDEN, D_MODEL), FFN_HIDDEN),
    }

def second_block(x, norm1_w, w_in, q_norm_w, k_norm_w, w_ret_out, w_moba_out, w_o,
              norm2_w, w_ffn_gate, w_ffn_up, w_ffn_down):
    B, S, _ = x.shape
    pos = jnp.arange(S)
    split_points = [int(v) for v in np.cumsum(IN_SPLITS)[:-1]]
    for l in range(DEPTH_2):
        h = rmsnorm(x, norm1_w[l])
        proj = h @ w_in[l]
        rq, rk, rv, rg, mq, mk, mv, ga, gb = jnp.split(proj, split_points, axis=-1)

        rq = rotary(rq.reshape(B, S, RET_HEADS, RET_DK), pos)
        rk = rotary(rk.reshape(B, S, RET_HEADS, RET_DK), pos) * (RET_DK ** -0.5)
        rv = rv.reshape(B, S, RET_HEADS, RET_DV)
        ret = jax.nn.silu(rg) * retention(rq, rk, rv)
        a = ret @ w_ret_out[l]

        mq = rmsnorm(mq.reshape(B, S, MOBA_HEADS, MOBA_DH), q_norm_w[l])
        mk = rmsnorm(mk.reshape(B, S, MOBA_HEADS, MOBA_DH), k_norm_w[l])
        mv = mv.reshape(B, S, MOBA_HEADS, MOBA_DH)
        b = moba_attention(mq, mk, mv) @ w_moba_out[l]

        mix = jax.nn.sigmoid(ga) * a + jax.nn.sigmoid(gb) * b
        x = x + mix @ w_o[l]

        h2 = rmsnorm(x, norm2_w[l])
        f = (jax.nn.silu(h2 @ w_ffn_gate[l]) * (h2 @ w_ffn_up[l])) @ w_ffn_down[l]
        x = x + f
    return x


def setup_inputs(seed=0):
    out = dict(first_inputs(seed))
    for name, value in second_inputs(seed + 1).items():
        if name != "x":
            out[name + "_2"] = value
    return out


def reference(
    x, norm_mix_g, norm_ffn_g, ev_w_in, ev_w_out, ev_q_norm_g, ev_k_norm_g, ev_pool_w,
    ev_pool_scale, od_w_qkv, od_w_out, ffn_w1, ffn_w3, ffn_w2, norm1_w_2, w_in_2, q_norm_w_2,
    k_norm_w_2, w_ret_out_2, w_moba_out_2, w_o_2, norm2_w_2, w_ffn_gate_2, w_ffn_up_2,
    w_ffn_down_2,
):
    x = first_block(
        x, norm_mix_g, norm_ffn_g, ev_w_in, ev_w_out, ev_q_norm_g, ev_k_norm_g, ev_pool_w,
        ev_pool_scale, od_w_qkv, od_w_out, ffn_w1, ffn_w3, ffn_w2,
    )
    return second_block(
        x, norm1_w_2, w_in_2, q_norm_w_2, k_norm_w_2, w_ret_out_2, w_moba_out_2, w_o_2,
        norm2_w_2, w_ffn_gate_2, w_ffn_up_2, w_ffn_down_2,
    )


_drawn_inputs = setup_inputs


def setup_inputs(seed=0):
    import zlib

    import numpy as np

    out = dict(_drawn_inputs(seed))
    spreads = {}
    factors = {'ev_q_norm_g': 5.926,
     'ev_k_norm_g': 5.84,
     'norm1_w_2': 6.104,
     'q_norm_w_2': 8.0,
     'k_norm_w_2': 8.0,
     'norm2_w_2': 5.477}
    for name, (base, spread) in spreads.items():
        noise = np.random.default_rng([zlib.crc32(name.encode()), seed]).standard_normal(out[name].shape)
        drawn = base * np.exp(spread * noise) if base else spread * noise
        out[name] = __import__('jax').numpy.asarray(drawn.astype(out[name].dtype))
    for name, factor in factors.items():
        out[name] = (out[name] * factor).astype(out[name].dtype)
    return out
```

```python
from contextlib import ExitStack

import concourse.bass as bass
from concourse import mybir
import numpy as np

F32 = mybir.dt.float32
F32R = mybir.dt.float32r
ALU = mybir.AluOpType
ACT = mybir.ActivationFunctionType
AX_X = mybir.AxisListType.X

P = 128
SEQ = 256
NT = SEQ // P
D = 1024
KD = D // P
HD = 64
FF = 2816
FC = 256
FSTEPS = FF // FC
EPS = 1e-6
GN_EPS = 1e-5
N_SEL = 64
IDX_HEADS = 4
IDX_SCALE = (IDX_HEADS * HD) ** -0.5
QK_SCALE = HD ** -0.5
RET_HEADS = 4
RET_DV = 256
RET_SCALE = 128 ** -0.5
MASKED = -(2.0 ** 100)
TAKEN = -(2.0 ** 127)
TRI = P + SEQ
UNIT = 2048
RING = 3
SET_A, SET_B = (0, 1), (2, 3)
TALL_MID, TALL_LOW, TALL_ENDS = (2, 3, 4, 5), (0, 1, 2, 3), (6, 7, 0, 1)
XT_BANKS = ((6, 7), (2, 3))
E_LB, M_LB = (0, 1), (4, 5)
PT_BANK, PV_BANK = 6, 7

CONST_COLS = {}
_at = 0
for _name, _n in (("ident", P), ("tri_neg", P), ("ones_neg", P), ("causal", TRI), ("strict", P),
                  ("rope", NT * 2 * P), ("bands", 4 * TRI), ("decay", RET_HEADS * TRI)):
    CONST_COLS[_name] = (_at, _n)
    _at += _n
CONST_N = _at


def constants():
    c = np.zeros((P, CONST_N), np.float32)

    def put(name, a):
        at, n = CONST_COLS[name]
        c[:, at:at + n] = np.asarray(a, np.float32).reshape(P, n)

    i = np.arange(P)
    put("ident", np.eye(P))
    put("tri_neg", np.where(i[:, None] >= i[None, :], -1.0, 0.0))
    put("ones_neg", -np.ones((P, P)))
    causal = np.where(i[None, :] <= i[:, None], 0.0, MASKED)
    put("causal", np.concatenate([causal, np.zeros((P, P)), causal], 1))
    put("strict", np.where(i[:, None] < i[None, :], 0.0, MASKED))
    t = np.arange(SEQ)
    src, dst = t[:, None], t[None, :]
    bands = []
    for w in (2, 4, 8, 16):
        full = np.where((dst >= src) & (dst - src < w), 1.0 / np.minimum(dst + 1, w), 0.0) - np.eye(SEQ)
        bands.append(np.concatenate([full[:P], full[P:, P:]], 1))
    put("bands", np.stack(bands, 1))
    lg = np.log1p(-np.exp2(-5.0 - np.arange(RET_HEADS)))
    decay = []
    for h in range(RET_HEADS):
        full = np.where(dst >= src, np.exp(np.maximum(dst - src, 0) * lg[h]), 0.0)
        decay.append(np.concatenate([full[:P], full[P:, P:]], 1))
    put("decay", np.stack(decay, 1))
    inv = np.float32(10000.0) ** (-np.arange(HD, dtype=np.float32) / np.float32(HD))
    ang = (t.astype(np.float32)[:, None] * inv[None, :]).astype(np.float32).reshape(NT, P, HD)
    cos, sin = np.cos(ang), np.sin(ang)
    rope = np.stack([np.concatenate([cos, cos], 2), np.concatenate([-sin, sin], 2)], 1)
    put("rope", rope.transpose(2, 0, 1, 3))
    return c


def program(nc, x, norm_mix_g, norm_ffn_g, ev_w_in, ev_w_out, ev_q_norm_g, ev_k_norm_g, ev_pool_w,
            ev_pool_scale, od_w_qkv, od_w_out, ffn_w1, ffn_w3, ffn_w2, norm1_w_2, w_in_2, q_norm_w_2,
            k_norm_w_2, w_ret_out_2, w_moba_out_2, w_o_2, norm2_w_2, w_ffn_gate_2, w_ffn_up_2,
            w_ffn_down_2, consts, out):
    def wide_src(w, c0, n, k0):
        return [(2 * j, n, w[(k0 + 2 * j) * P:(k0 + 2 * j + 2) * P, c0:c0 + n]) for j in range(2)]

    units = []

    def add_wide(w, c0, n=512):
        at = len(units)
        units.extend([wide_src(w, c0, n, 0), wide_src(w, c0, n, 4)])
        return at

    def add_tall(w, pairs):
        at = len(units)
        for p in pairs:
            units.append([(j, D, w[(2 * p + j) * P:(2 * p + j + 1) * P, :]) for j in range(2)])
        return at

    def add_ffn():
        at = len(units)
        units.extend([None] * (3 * FSTEPS))
        return at

    w0 = ev_w_in[0]
    KI_COLS = HD + IDX_HEADS
    U_KI = add_wide(w0, 1024, KI_COLS)
    U_KVQI = add_wide(w0, 512)
    U_Q = add_wide(w0, 0)
    U_POOL = add_wide(w0, 1024 + KI_COLS)
    U_EOUT = add_tall(ev_w_out[0], (2, 3, 0, 1))
    U_FFN = [add_ffn()]
    U_QKV = [add_wide(od_w_qkv[0], 1024 * part + 512 * half) for half in range(2) for part in range(3)]
    U_OOUT = add_tall(od_w_out[0], range(4))
    U_FFN.append(add_ffn())
    W2 = w_in_2[0]
    P2_COLS = (3072, 3584, 4096, 0, 512, 1024, 1536, 2048, 2560, 4608, 5120, 5632, 6144)
    U_P2 = [add_wide(W2, c) for c in P2_COLS]
    U_MOBA = add_tall(w_moba_out_2[0], range(2))
    U_RET = add_tall(w_ret_out_2[0], range(4))
    U_WO = add_tall(w_o_2[0], range(4))
    U_FFN.append(add_ffn())
    N_UNITS = len(units)
    FFN_W = [(ffn_w1[0], ffn_w3[0], ffn_w2[0]), (ffn_w1[1], ffn_w3[1], ffn_w2[1]),
             (w_ffn_gate_2[0], w_ffn_up_2[0], w_ffn_down_2[0])]
    NORM_G = [norm_mix_g[0], norm_ffn_g[0], norm_mix_g[1], norm_ffn_g[1], norm1_w_2[0], None, norm2_w_2[0]]

    with ExitStack() as ctx:
        def sb(name, shape, dt=F32):
            return ctx.enter_context(nc.sbuf_tensor(name, shape, dt))

        def sem(name):
            return ctx.enter_context(nc.semaphore(name))

        raw = sb("raw", [P, RING, UNIT])
        high = sb("high", [P, RING, UNIT], F32R)
        low = sb("low", [P, RING, UNIT], F32R)
        xs = sb("xs", [P, NT, D])
        xn = sb("xn", [P, NT, D])
        xh = sb("xh", [P, KD, SEQ], F32R)
        xl = sb("xl", [P, KD, SEQ], F32R)
        mh = sb("mh", [P, KD, SEQ], F32R)
        ml = sb("ml", [P, KD, SEQ], F32R)
        gains = sb("gains", [P, D])
        gh = sb("gh", [P, 2, SEQ], F32R)
        gl = sb("gl", [P, 2, SEQ], F32R)
        arena = sb("arena", [P, 14 * 1024])
        DECAY_AT = CONST_COLS["decay"][0]
        cst = sb("cst", [P, DECAY_AT])
        identr = sb("identr", [P, P], F32R)
        causalr = sb("causalr", [P, TRI], F32R)
        strictr = sb("strictr", [P, P], F32R)
        selbias = sb("selbias", [P, TRI], F32R)
        poolw = sb("poolw", [P, 4, P])
        small = sb("small", [P, 256])
        psum = ctx.enter_context(nc.psum_tensor("psum", [P, 8, 512], F32))

        def const(name):
            at, n = CONST_COLS[name]
            return cst[:, at:at + n]

        ident, tri_neg, ones_neg = const("ident"), const("tri_neg"), const("ones_neg")
        causal = const("causal")
        bands = const("bands").rearrange("p (g n) -> p g n", g=4)
        decay = bands
        rope = const("rope").rearrange("p (t c d) -> p t c d", t=NT, c=2)

        sumsq = small[:, 0:14]
        msq = small[:, 14:28]
        rstd = small[:, 28:42]
        head_ss = small[:, 48:112].rearrange("p (e h) -> p e h", h=8)
        head_ms = small[:, 112:176].rearrange("p (e h) -> p e h", h=8)
        neg_half = small[:, 176:184]
        head_gain = small[:, 184:188]
        q_gain = small[:, 188:190]
        pool_gain = small[:, 190:194]
        row_max = small[:, 194:198].rearrange("p (b t) -> p b t", t=NT)
        row_sum = small[:, 198:202].rearrange("p (b t) -> p b t", t=NT)
        row_inv = small[:, 202:206].rearrange("p (b t) -> p b t", t=NT)
        top8 = small[:, 206:214]
        idx_w = small[:, 214:222].rearrange("p (t h) -> p t h", t=NT)
        gn_mv = small[:, 222:238].rearrange("p (t h s) -> p t h s", t=NT, h=RET_HEADS)
        gn_rstd = small[:, 238:246].rearrange("p (t h) -> p t h", t=NT)
        gn_var = small[:, 246:254].rearrange("p (t h) -> p t h", t=NT)
        head_rs = sb("head_rs", [P, 8, 8])
        gn_stats = sb("gn_stats", [P, NT, RET_HEADS, 6])

        class Carve:
            def __init__(self, at=0):
                self.at = at

            def __call__(self, n):
                self.at += n
                assert self.at <= 14 * 1024, self.at
                return arena[:, self.at - n:self.at]

        def blocks(ap, n):
            return ap.rearrange("p (t n) -> p t n", t=n)

        take = Carve()
        f_silu, f_hidden = blocks(take(NT * FC), NT), blocks(take(NT * FC), NT)
        take = Carve()
        probs, probsT = blocks(take(2 * TRI), 2), blocks(take(2 * TRI), 2)
        SOFTMAX_END = take.at
        e_sq = blocks(take(NT * 512), NT)
        e_kk = blocks(take(NT * P), NT)
        e_vqi = blocks(take(NT * 384), NT)
        e_kn = blocks(take(NT * P), NT)
        e_qn = blocks(take(NT * 512), NT)
        e_kiT = take(SEQ)
        e_kT = take(SEQ)
        e_qiT = blocks(take(2 * SEQ), 2)
        e_qT = blocks(take(4 * SEQ), 4)
        e_u = blocks(take(NT * 512), NT)
        e_pm = blocks(take(4 * SEQ), 4)
        e_rel = take(NT * 4 * SEQ).rearrange("p (t h k) -> p t h k", t=NT, h=IDX_HEADS)
        e_score = take(SEQ)
        e_hit = take(SEQ)
        take = Carve()
        o_tok = take(4 * 512).rearrange("p (b t n) -> p b t n", b=2, t=NT)
        o_qT = take(8 * SEQ).rearrange("p (f j t) -> p f j t", f=2, j=4)
        o_kT = take(8 * SEQ).rearrange("p (f j t) -> p f j t", f=2, j=4)
        o_v = take(4 * 512).rearrange("p (f t n) -> p f t n", f=2, t=NT)
        o_log = take(2 * TRI).rearrange("p (e n) -> p e n", e=2)
        o_brk = take(4 * TRI).rearrange("p (b e n) -> p b e n", b=2, e=2)
        o_a = take(4 * TRI).rearrange("p (b e n) -> p b e n", b=2, e=2)
        take = Carve(SOFTMAX_END)
        m_sq = blocks(take(NT * 512), NT)
        m_tok = blocks(take(NT * 512), NT)
        gate_a = blocks(take(NT * D), NT)
        m_qT = gate_a[:, 0, :].rearrange("p (j t) -> p j t", j=4)
        m_kT = gate_a[:, 1, :].rearrange("p (j t) -> p j t", j=4)
        m_v = blocks(take(NT * 512), NT)
        gate_b = blocks(take(NT * D), NT)
        r_qT = gate_b[:, 0, :].rearrange("p (j t) -> p j t", j=4)
        r_kT = gate_b[:, 1, :].rearrange("p (j t) -> p j t", j=4)
        r_v = blocks(take(NT * D), NT)
        r_gate = blocks(take(NT * D), NT)
        r_tok = xn[:, :, :].rearrange("p t (b n) -> p b t n", b=2)
        r_half = m_sq
        r_a = blocks(take(RET_HEADS * TRI), RET_HEADS)
        r_o = xn

        consts_in = sem("consts_in")
        x_in = sem("x_in")
        gains_in = sem("gains_in")
        small_in = sem("small_in")
        landed = [sem(f"landed{i}") for i in range(RING)]
        high_ready, low_ready, unit_used = sem("high_ready"), sem("low_ready"), sem("unit_used")
        masks_ready = sem("masks_ready")
        half_ready = sem("half_ready")
        q_gain_ready = sem("q_gain_ready")
        sumsq_ready, msq_ready, rstd_ready = sem("sumsq_ready"), sem("msq_ready"), sem("rstd_ready")
        xn_ready, xT_ready, xh_ready, xl_ready = sem("xn_ready"), sem("xT_ready"), sem("xh_ready"), sem("xl_ready")
        x_added = sem("x_added")
        wide_ready = [sem("wide_ready_a"), sem("wide_ready_b")]
        silu_ready, hidden_ready = sem("silu_ready"), sem("hidden_ready")
        hiddenT_ready, gh_ready, gl_ready = sem("hiddenT_ready"), sem("gh_ready"), sem("gl_ready")
        head_sq, head_sum, head_ms_ready = sem("head_sq"), sem("head_sum"), sem("head_ms_ready")
        head_rs_ready, head_normed = sem("head_rs_ready"), sem("head_normed")
        headT_ready, headT_copied = sem("headT_ready"), sem("headT_copied")
        ki_copied, vqi_copied, idx_w_copied = sem("ki_copied"), sem("vqi_copied"), sem("idx_w_copied")
        kiT_ready, qiT_ready, kiT_copied, qiT_copied = sem("kiT_ready"), sem("qiT_ready"), sem("kiT_copied"), sem("qiT_copied")
        idx_ready, rel_ready, topk_step, sel_ready = sem("idx_ready"), sem("rel_ready"), sem("topk_step"), sem("sel_ready")
        u_copied, pooled_ready, pooled_copied = sem("u_copied"), sem("pooled_ready"), sem("pooled_copied")
        poolmix_ready, poolmix_high, poolmix_low = sem("poolmix_ready"), sem("poolmix_high"), sem("poolmix_low")
        logits_ready, max_ready, exp_ready, inv_ready = sem("logits_ready"), sem("max_ready"), sem("exp_ready"), sem("inv_ready")
        probs_ready, probsT_ready, probsT_copied = sem("probs_ready"), sem("probsT_ready"), sem("probsT_copied")
        pv_ready, pv_high, pv_low = sem("pv_ready"), sem("pv_high"), sem("pv_low")
        qkv_copied, qkvT_ready, qkvT_copied, v_copied = sem("qkv_copied"), sem("qkvT_ready"), sem("qkvT_copied"), sem("v_copied")
        z_ready, abs_ready, e_ready, log_ready = sem("z_ready"), sem("abs_ready"), sem("e_ready"), sem("log_ready")
        brk_ready, loga_ready, a_ready = sem("brk_ready"), sem("loga_ready"), sem("a_ready")
        sbv_ready, sbv_high, sbv_low = sem("sbv_ready"), sem("sbv_high"), sem("sbv_low")
        mv_copied, rv_copied, rg_ready = sem("mv_copied"), sem("rv_copied"), sem("rg_ready")
        gates_ready = sem("gates_ready")
        rope_step, roped = sem("rope_step"), sem("roped")
        ropeT_ready, ropeT_copied = sem("ropeT_ready"), sem("ropeT_copied")
        rscore_ready, decayed, ro_ready = sem("rscore_ready"), sem("decayed"), sem("ro_ready")
        gn_step, gn_var_ready, gn_rstd_ready, gn_done = sem("gn_step"), sem("gn_var_ready"), sem("gn_rstd_ready"), sem("gn_done")
        ret_ready, retT_ready, ret_high, ret_low = sem("ret_ready"), sem("retT_ready"), sem("ret_high"), sem("ret_low")
        b_gated, a_gated = sem("b_gated"), sem("a_gated")
        stored = sem("stored")

        def bank(b, c0=0, c1=512):
            return psum[:, b, c0:c1]

        def slot_tile(ring, n, k, cols):
            return ring[:, n % RING, k * cols:(k + 1) * cols]

        wide_chunks = [(U_KI, 0, [(idx_w_copied, 2)]), (U_KVQI, 1, [(vqi_copied, 2), (head_normed, 2)]),
                       (U_Q, 0, [(head_normed, 4)]), (U_POOL, 1, [(u_copied, 2)])]
        for c, u in enumerate(U_QKV):
            half, part = divmod(c, 3)
            read = [(v_copied, 2 * half + 2)] if part == 2 else [(qkv_copied, 4 * half + 2 * part + 2)]
            wide_chunks.append((u, c % 2, read))
        P2_READS = [(head_normed, 6), (head_normed, 8), (mv_copied, 2), (roped, 2), (roped, 4), (rv_copied, 2),
                    (rv_copied, 4), (rg_ready, 2), (rg_ready, 4), (gates_ready, 2), (gates_ready, 4),
                    (gates_ready, 6), (gates_ready, 8)]
        wide_chunks += [(u, c % 2, [P2_READS[c]]) for c, u in enumerate(U_P2)]

        def reads_before(unit):
            s = chunk_set(unit)
            earlier = [reads for u, ss, reads in wide_chunks if ss == s and u < unit]
            return earlier[-1] if earlier else []

        def chunk_set(unit):
            return next(s for u, s, _ in wide_chunks if u == unit)

        def chunk_done(eng, unit, t):
            if t:
                eng.wait_ge(unit_used, unit + 2)
            else:
                s = chunk_set(unit)
                before = sum(1 for u, ss, _ in wide_chunks if ss == s and u < unit)
                steps = FSTEPS * sum(1 for u in U_FFN if u < unit) if s == 0 else 0
                eng.wait_ge(wide_ready[s], before + steps + 1)

        def step_done(eng, f, c, t):
            if t:
                eng.wait_ge(unit_used, U_FFN[f] + (3 * c + 1 if c_late(c) else 2))
            else:
                before = sum(1 for u, ss, _ in wide_chunks if ss == 0 and u < U_FFN[f])
                eng.wait_ge(wide_ready[0], before + FSTEPS * f + c + 1)

        def c_late(c):
            return not isinstance(c, int) or c > 0

        block = ctx.enter_context(nc.Block())

        @block.sync
        def _(sp):
            def load(n):
                if n >= RING:
                    sp.wait_ge(low_ready, n - RING + 1)
                for k0, cols, src in units[n]:
                    rows = src.shape[0] // P
                    dst = raw[:, n % RING, k0 * cols:(k0 + rows) * cols].rearrange("p (k c) -> p k c", k=rows)
                    sp.dma_start(dst, src.rearrange("(k p) c -> p k c", p=P)).then_inc(landed[n % RING], 16)

            def load_up(f, n, c, k0, after):
                sp.wait_ge(low_ready, after)
                dst = raw[:, n % RING, :].rearrange("p (k c) -> p k c", k=4)
                for j in range(2):
                    src = FFN_W[f][j][k0 * P:(k0 + 4) * P, bass.ds(c * FC, FC)]
                    sp.dma_start(dst[:, :, j * FC:(j + 1) * FC], src.rearrange("(k p) c -> p k c", p=P)
                                 ).then_inc(landed[n % RING], 16)

            def load_down(f, n, c, after):
                sp.wait_ge(low_ready, after)
                for j in range(2):
                    sp.dma_start(raw[:, n % RING, j * D:(j + 1) * D], FFN_W[f][2][bass.ds(c * FC + j * P, P), :]
                                 ).then_inc(landed[n % RING], 16)

            def load_ffn(f):
                n0 = U_FFN[f]
                load_up(f, n0, 0, 0, n0 - RING + 1)
                load_up(f, n0 + 1, 0, 4, n0 + 1 - RING + 1)
                n = n0 + 2
                with sp.Fori(0, FSTEPS - 1) as i:
                    load_up(f, n, i + 1, 0, n - RING + 1 + 3 * i)
                    load_up(f, n + 1, i + 1, 4, n + 1 - RING + 1 + 3 * i)
                    load_down(f, n + 2, i, n + 2 - RING + 1 + 3 * i)
                n = n0 + 3 * FSTEPS - 1
                load_down(f, n, FSTEPS - 1, n - RING + 1)

            for t in range(NT):
                sp.dma_start(xs[:, t, :], x[0, t * P:(t + 1) * P, :]).then_inc(x_in, 16)
            n = 0
            while n < N_UNITS:
                if n in U_FFN:
                    load_ffn(U_FFN.index(n))
                    n += 3 * FSTEPS
                else:
                    load(n)
                    n += 1
            for t in range(NT):
                sp.wait_ge(x_added, 6 * NT - NT + t + 1)
                sp.dma_start(out[0, t * P:(t + 1) * P, :], xs[:, t, :]).then_inc(stored, 16)
            sp.wait_ge(stored, 16 * NT)

        @block.gpsimd
        def _(pool):
            pool.dma_start(cst[:], consts[:, 0:DECAY_AT]).then_inc(consts_in, 16)

            def load_gain(k, m):
                if m >= 1:
                    pool.wait_ge(xn_ready, 2 * k_before[m])
                pool.dma_start(gains[:], NORM_G[k].partition_broadcast(P)).then_inc(gains_in, 16)

            norm_ks = [k for k in range(7) if NORM_G[k] is not None]
            k_before = {m: norm_ks[m - 1] + 1 for m in range(1, len(norm_ks))}
            load_gain(0, 0)
            with nc.allow_non_contiguous_dma(reason="gains of a head: one element per partition"):
                for i, g in enumerate((ev_q_norm_g, ev_k_norm_g, q_norm_w_2, k_norm_w_2)):
                    for r in range(2):
                        pool.dma_start(head_gain[r * HD:(r + 1) * HD, i:i + 1],
                                       g[0].rearrange("(p o) -> p o", o=1)).then_inc(small_in, 16)
                pool.dma_start(pool_gain, ev_pool_scale[0].rearrange("(g p) -> p g", p=P)).then_inc(small_in, 16)
            pool.dma_start(poolw[:], ev_pool_w[0].rearrange("g c d -> c g d")).then_inc(small_in, 16)
            nc.gpsimd.memset(neg_half, -0.5).then_inc(half_ready, 1)
            pool.wait_ge(half_ready, 1)

            def row_rstd(k, e):
                for t in range(NT):
                    i = 2 * k + t
                    pool.wait_ge(sumsq_ready, 2 * e + t + 1)
                    nc.gpsimd.tensor_scalar(msq[:, i:i + 1], sumsq[:, i:i + 1], 1.0 / D, EPS,
                                            ALU.mult, ALU.add).then_inc(msq_ready, 1)
                    pool.wait_ge(msq_ready, 2 * e + t + 1)
                    nc.gpsimd.tensor_tensor(rstd[:, i:i + 1], msq[:, i:i + 1], neg_half[:, 0:1],
                                            ALU.pow).then_inc(rstd_ready, 1)

            def head_rstd(events, n):
                for e in events:
                    pool.wait_ge(head_sum, e + 1)
                    nc.gpsimd.tensor_scalar(head_ms[:, e, 0:n], head_ss[:, e, 0:n], 1.0 / HD, EPS,
                                            ALU.mult, ALU.add).then_inc(head_ms_ready, 1)
                    pool.wait_ge(head_ms_ready, e + 1)
                    nc.gpsimd.tensor_tensor(head_rs[:, e, 0:n], head_ms[:, e, 0:n], neg_half[:, 0:n],
                                            ALU.pow).then_inc(head_rs_ready, 1)

            row_rstd(0, 0)
            load_gain(1, 1)
            head_rstd((0, 1), 2)
            head_rstd((2, 3), 8)
            for e in (1, 2, 3, 4):
                row_rstd(e, e)
                if e == 1:
                    pool.wait_ge(pooled_ready, 1)
                    pool.dma_start(cst[:, CONST_COLS["bands"][0]:DECAY_AT], consts[:, DECAY_AT:]
                                   ).then_inc(consts_in, 16)
                load_gain(norm_ks[e + 1], e + 1)
            head_rstd((4, 5, 6, 7), 8)
            for t in range(NT):
                pool.wait_ge(gn_var_ready, t + 1)
                nc.gpsimd.tensor_scalar(gn_var[:, t, :], gn_mv[:, t, :, 1], 1.0, GN_EPS,
                                        ALU.mult, ALU.add).then_inc(gn_step, 1)
                pool.wait_ge(gn_step, t + 1)
                nc.gpsimd.tensor_tensor(gn_rstd[:, t, :], gn_var[:, t, :], neg_half[:, 0:RET_HEADS],
                                        ALU.pow).then_inc(gn_rstd_ready, 1)
            row_rstd(6, 5)

        @block.scalar
        def _(act):
            def split_high(n, i=0):
                if isinstance(i, int) and n + 3 * i >= N_UNITS:
                    return
                cols = sum(s.shape[0] // P * c for _, c, s in units[n]) if n < N_UNITS and units[n] else UNIT
                act.wait_ge(landed[n % RING], 32 * (n // RING + 1) + 32 * i)
                if n >= RING:
                    act.wait_ge(unit_used, n - RING + 1 + 3 * i)
                nc.scalar.activation(high[:, n % RING, 0:cols], raw[:, n % RING, 0:cols], ACT.Copy
                                     ).then_inc(high_ready, 1)

            def row_squares(k, e):
                for t in range(NT):
                    if e:
                        act.wait_ge(x_added, 2 * (e - 1) + t + 1)
                    else:
                        act.wait_ge(x_in, 16 * NT)
                    i = 2 * k + t
                    nc.scalar.activation(xn[:, t, :], xs[:, t, :], ACT.Square, accum_out=sumsq[:, i:i + 1]
                                         ).then_inc(sumsq_ready, 1)

            def xT_high(k, dst):
                for t in range(NT):
                    for q in range(2):
                        act.wait_ge(xT_ready, 4 * k + 2 * t + q + 1)
                        nc.scalar.activation(dst[:, 4 * q:4 * q + 4, t * P:(t + 1) * P],
                                             bank(XT_BANKS[t][q]).rearrange("p (k n) -> p k n", k=4), ACT.Copy
                                             ).then_inc(xh_ready, 1)

            def head_squares(unit, events, n):
                for t, e in enumerate(events):
                    chunk_done(act, unit, t)
                    if e >= 2:
                        act.wait_ge(head_sum, e - 1)
                    sq = (e_sq if e < 4 else m_sq)[:, t, 0:n]
                    nc.scalar.activation(sq, bank((SET_A, SET_B)[chunk_set(unit)][t], 0, n), ACT.Square
                                         ).then_inc(head_sq, 1)

            def headT_copy(event, dst, src, gain):
                act.wait_ge(headT_ready, event)
                nc.scalar.activation(dst, src, ACT.Copy, scale=gain).then_inc(headT_copied, 1)

            def copy_chunk(unit, t, dst, done, func=ACT.Copy, scale=1.0):
                chunk_done(act, unit, t)
                nc.scalar.activation(dst, bank((SET_A, SET_B)[chunk_set(unit)][t]), func, scale=scale).then_inc(done, 1)

            def softmax_exp(a, h, lb):
                act.wait_ge(max_ready, 2 * (8 * a + h) + 2)
                if h >= 2:
                    act.wait_ge(probsT_ready, 8 * a + h - 1)
                b = h % 2
                for t, (c0, c1) in enumerate(((0, P), (P, TRI))):
                    nc.scalar.activation(probs[:, b, c0:c1], bank(lb[b], c0, c1), ACT.Exp,
                                         bias=row_max[:, b, t:t + 1], accum_out=row_sum[:, b, t:t + 1]
                                         ).then_inc(exp_ready, 1)

            def softmax_T(a, h):
                act.wait_ge(probsT_ready, 8 * a + h + 1)
                if h >= 2:
                    act.wait_ge(pv_ready, 8 * a + h - 1)
                nc.scalar.activation(probsT[:, h % 2, :], bank(PT_BANK, 0, TRI), ACT.Copy).then_inc(probsT_copied, 1)

            def softmax_out(a, j):
                act.wait_ge(pv_ready, 8 * a + 2 * j + 2)
                nc.scalar.activation(mh[:, j, :], bank(PV_BANK, 0, SEQ), ACT.Copy).then_inc(pv_high, 1)

            def softmax_start(a, lb):
                softmax_exp(a, 0, lb)
                softmax_exp(a, 1, lb)

            def softmax_head(a, h, lb):
                softmax_T(a, h)
                if h + 2 < 8:
                    softmax_exp(a, h + 2, lb)
                if h % 2:
                    softmax_out(a, h // 2)

            def ffn(f):
                n0 = U_FFN[f]

                def gated(c):
                    for t in range(NT):
                        step_done(act, f, c, t)
                        if f or c_late(c):
                            act.wait_ge(hidden_ready, 2 * (FSTEPS * f + c) - 1 + t)
                        nc.scalar.activation(f_silu[:, t, :], bank(SET_A[t], 0, FC), ACT.Silu).then_inc(silu_ready, 1)

                def hiddenT(c):
                    act.wait_ge(hiddenT_ready, FSTEPS * f + c + 1)
                    if f or c_late(c):
                        act.wait_ge(unit_used, n0 + 2 + 3 * c)
                    nc.scalar.activation(gh[:], bank(6).rearrange("p (k n) -> p k n", k=2), ACT.Copy).then_inc(gh_ready, 1)

                def step(c, i):
                    n = n0 + 2
                    split_high(n + 3, i)
                    hiddenT(c - 1)
                    gated(c)
                    split_high(n + 4, i)
                    split_high(n + 5, i)

                split_high(n0 + 3)
                gated(0)
                split_high(n0 + 4)
                step(1, 0)
                ahead = 0 if n0 + 3 * FSTEPS < N_UNITS else 1
                with act.Fori(1, FSTEPS - 1 - ahead) as i:
                    step(i + 1, i)
                if ahead:
                    step(FSTEPS - 1, FSTEPS - 2)
                hiddenT(FSTEPS - 1)
                split_high(n0 + 3 * FSTEPS + 2)

            row_squares(0, 0)
            act.wait_ge(consts_in, 16)
            nc.scalar.activation(identr[:], ident, ACT.Copy).then_inc(masks_ready, 1)
            nc.scalar.activation(causalr[:], causal, ACT.Copy).then_inc(masks_ready, 1)
            nc.scalar.activation(strictr[:], const("strict"), ACT.Copy).then_inc(masks_ready, 1)
            for n in range(RING):
                split_high(n)
            xT_high(0, xh)

            split_high(U_KI + 3)
            split_high(U_KI + 4)
            for t in range(NT):
                chunk_done(act, U_KI, t)
                nc.scalar.activation(e_kk[:, t, :].rearrange("p (r d) -> p r d", r=2),
                                     bank(SET_A[t], 0, HD).unsqueeze(1).to_broadcast([P, 2, HD]), ACT.Copy
                                     ).then_inc(ki_copied, 1)
                nc.scalar.activation(idx_w[:, t, :], bank(SET_A[t], HD, KI_COLS), ACT.Copy, scale=IDX_SCALE
                                     ).then_inc(idx_w_copied, 1)
            split_high(U_KI + 5)
            head_squares(U_KVQI, (0, 1), P)
            for t in range(NT):
                nc.scalar.activation(e_vqi[:, t, :], bank(SET_B[t], P, 512), ACT.Copy).then_inc(vqi_copied, 1)
            split_high(U_KI + 6)
            act.wait_ge(small_in, 16 * 10)
            headT_copy(1, e_kT, bank(6, 0, SEQ), head_gain[:, 1:2])
            split_high(U_KI + 7)
            head_squares(U_Q, (2, 3), 512)
            split_high(U_KI + 8)
            for t in range(NT):
                act.wait_ge(idx_ready, t + 1)
                k = (t + 1) * P
                nc.scalar.activation(e_rel[:, t, :, 0:k].rearrange("p (j b) k -> p b j k", b=2),
                                     psum[:, 4 + 2 * t:6 + 2 * t, 0:2 * k].rearrange("p b (j k) -> p b j k", j=2),
                                     ACT.Relu).then_inc(rel_ready, 1)
            split_high(U_KI + 9)
            act.wait_ge(q_gain_ready, 1)
            for t in range(NT):
                headT_copy(2 + t, e_qT[:, :, t * P:(t + 1) * P], bank(4 + t).rearrange("p (j n) -> p j n", j=4),
                           q_gain[:, 0:1])
            for t in range(NT):
                copy_chunk(U_POOL, t, e_u[:, t, :], u_copied)
            split_high(U_KI + 10)
            act.wait_ge(pooled_ready, 1)
            nc.scalar.activation(e_pm.rearrange("p (b j) n -> p b (j n)", b=2), psum[:, 0:2, :], ACT.Copy).then_inc(pooled_copied, 1)
            for g in range(4):
                act.wait_ge(poolmix_ready, 1)
                nc.scalar.activation(mh[:, 4 + g, :], bank(2 + g // 2, (g % 2) * SEQ, (g % 2 + 1) * SEQ), ACT.Copy,
                                     scale=pool_gain[:, g:g + 1]).then_inc(poolmix_high, 1)
            split_high(U_EOUT + 3)
            split_high(U_EOUT + 4)
            softmax_start(0, E_LB)
            for h in range(8):
                softmax_head(0, h, E_LB)
            split_high(U_EOUT + 5)
            split_high(U_EOUT + 6)
            row_squares(1, 1)
            xT_high(1, xh)
            ffn(0)

            row_squares(2, 2)
            xT_high(2, xh)

            def copy_T(half, f):
                for t in range(NT):
                    act.wait_ge(qkvT_ready, 4 * half + 2 * f + t + 1)
                    dst = (o_qT, o_kT)[f][:, half, :, t * P:(t + 1) * P]
                    nc.scalar.activation(dst, bank(4 + 2 * f + t).rearrange("p (j n) -> p j n", j=4), ACT.Copy
                                         ).then_inc(qkvT_copied, 1)

            def stick_exp(p):
                act.wait_ge(z_ready, p + 1)
                if p:
                    act.wait_ge(brk_ready, p)
                b = 4 + 2 * (p % 2)
                nc.scalar.activation(o_log, psum[:, b:b + 2, 0:TRI], ACT.Abs).then_inc(abs_ready, 1)
                act.wait_ge(abs_ready, p + 1)
                nc.scalar.activation(o_log, o_log, ACT.Exp, scale=-1.0).then_inc(e_ready, 1)
                act.wait_ge(e_ready, p + 1)
                nc.scalar.activation(o_log, o_log, ACT.Ln, bias=1.0).then_inc(log_ready, 1)

            def stick_a(p):
                act.wait_ge(loga_ready, p + 1)
                if p >= 2:
                    act.wait_ge(sbv_ready, p - 1)
                b = 4 + 2 * (p % 2)
                nc.scalar.activation(o_a[:, p % 2], psum[:, b:b + 2, 0:TRI], ACT.Exp).then_inc(a_ready, 1)

            def stick_out(p):
                act.wait_ge(sbv_ready, p + 1)
                b = 4 + 2 * (p % 2)
                nc.scalar.activation(mh[:, p, :].rearrange("p (t n) -> p t n", t=NT), psum[:, b:b + 2, TRI:512], ACT.Copy
                                     ).then_inc(sbv_high, 1)

            def stick_slot(s, first, n):
                if s >= 2:
                    stick_out(first + s - 2)
                if 1 <= s <= n:
                    stick_a(first + s - 1)
                if s < n:
                    stick_exp(first + s)

            U = U_QKV[0]
            for half in range(2):
                for j in range(6):
                    if j in (1, 3):
                        for t in range(NT):
                            f = j // 2
                            copy_chunk(U_QKV[3 * half + f], t, o_tok[:, f, t, :], qkv_copied, scale=(QK_SCALE, 1.0)[f])
                    if j == 5:
                        for t in range(NT):
                            copy_chunk(U_QKV[3 * half + 2], t, o_v[:, half, t, :], v_copied)
                    split_high(U + 6 * half + j + 3)
                    if half == 0:
                        if j == 2:
                            copy_T(0, 0)
                        if j == 4:
                            copy_T(0, 1)
                        if j == 5:
                            stick_slot(0, 0, 4)
                    else:
                        if j < 5:
                            stick_slot(j + 1, 0, 4)
                        if j == 4:
                            copy_T(1, 0)
                        if j == 5:
                            copy_T(1, 1)
            split_high(U_OOUT + 3)
            stick_slot(0, 4, 4)
            split_high(U_OOUT + 4)
            for s in range(1, 4):
                stick_slot(s, 4, 4)
            split_high(U_OOUT + 5)
            stick_slot(4, 4, 4)
            stick_slot(5, 4, 4)
            split_high(U_OOUT + 6)
            row_squares(3, 3)
            xT_high(3, xh)
            ffn(1)

            row_squares(4, 4)
            xT_high(4, xh)
            U = U_P2[0]
            for j in range(2 * len(U_P2)):
                c, last = divmod(j, 2)
                if last:
                    unit = U_P2[c]
                    if c < 2:
                        head_squares(unit, (4 + 2 * c, 5 + 2 * c), 512)
                    elif c == 2:
                        for t in range(NT):
                            copy_chunk(unit, t, m_v[:, t, :], mv_copied)
                    elif c in (5, 6):
                        for t in range(NT):
                            copy_chunk(unit, t, r_v[:, t, (c - 5) * 512:(c - 4) * 512], rv_copied)
                    elif c in (7, 8):
                        for t in range(NT):
                            copy_chunk(unit, t, r_gate[:, t, (c - 7) * 512:(c - 6) * 512], rg_ready, ACT.Silu)
                    elif c >= 9:
                        g, half = divmod(c - 9, 2)
                        if half == 0 and g == 0:
                            act.wait_ge(logits_ready, 16)
                        if half == 0 and g == 1:
                            act.wait_ge(rscore_ready, RET_HEADS)
                        for t in range(NT):
                            copy_chunk(unit, t, (gate_a, gate_b)[g][:, t, half * 512:(half + 1) * 512], gates_ready, ACT.Sigmoid)
                split_high(U + j + 3)
                if j == 3:
                    for t in range(NT):
                        headT_copy(4 + t, m_qT[:, :, t * P:(t + 1) * P], bank(4 + t).rearrange("p (j n) -> p j n", j=4),
                                   q_gain[:, 1:2])
                if j == 5:
                    for t in range(NT):
                        headT_copy(6 + t, m_kT[:, :, t * P:(t + 1) * P], bank(6 + t).rearrange("p (j n) -> p j n", j=4),
                                   head_gain[:, 3:4])
                if j == 6:
                    softmax_start(1, M_LB)
                if 7 <= j < 15:
                    softmax_head(1, j - 7, M_LB)
                if j in (16, 17):
                    for t in range(NT):
                        act.wait_ge(ropeT_ready, 2 * (j - 16) + t + 1)
                        nc.scalar.activation((r_qT, r_kT)[j - 16][:, :, t * P:(t + 1) * P],
                                             bank((4, 6)[j - 16] + t).rearrange("p (j n) -> p j n", j=4), ACT.Copy,
                                             scale=(1.0, RET_SCALE)[j - 16]).then_inc(ropeT_copied, 1)
            split_high(U_MOBA + 3)
            split_high(U_MOBA + 4)
            for t in range(NT):
                for q in range(2):
                    act.wait_ge(retT_ready, 2 * t + q + 1)
                    nc.scalar.activation(xh[:, 4 * q:4 * q + 4, t * P:(t + 1) * P],
                                         bank(2 + 2 * t + q).rearrange("p (k n) -> p k n", k=4), ACT.Copy).then_inc(ret_high, 1)
            for n in range(U_RET, U_WO):
                split_high(n + 3)
            xT_high(5, mh)
            for n in range(U_WO, U_FFN[2]):
                split_high(n + 3)
            row_squares(6, 5)
            xT_high(6, xh)
            ffn(2)

        @block.vector
        def _(dve):
            def split_low(n, i=0):
                if isinstance(i, int) and n + 3 * i >= N_UNITS:
                    return
                cols = sum(s.shape[0] // P * c for _, c, s in units[n]) if n < N_UNITS and units[n] else UNIT
                dve.wait_ge(high_ready, n + 1 + 3 * i)
                nc.vector.tensor_tensor(low[:, n % RING, 0:cols], raw[:, n % RING, 0:cols],
                                        high[:, n % RING, 0:cols].bitcast(F32), ALU.subtract).then_inc(low_ready, 1)

            def normalise(k, e, m):
                for t in range(NT):
                    i = 2 * k + t
                    dve.wait_ge(gains_in, 16 * (m + 1))
                    dve.wait_ge(rstd_ready, 2 * e + t + 1)
                    nc.vector.scalar_tensor_tensor(out=xn[:, t, :], in0=xs[:, t, :], scalar=rstd[:, i:i + 1],
                                                   in1=gains[:], op0=ALU.mult, op1=ALU.mult).then_inc(xn_ready, 1)

            def xT_low(k, hi, lo):
                for t in range(NT):
                    for q in range(2):
                        dve.wait_ge(xh_ready, 4 * k + 2 * t + q + 1)
                        s = (slice(None), slice(4 * q, 4 * q + 4), slice(t * P, (t + 1) * P))
                        nc.vector.tensor_tensor(lo[s], bank(XT_BANKS[t][q]).rearrange("p (k n) -> p k n", k=4),
                                                hi[s].bitcast(F32), ALU.subtract).then_inc(xl_ready, 1)

            def add_residual(end, banks):
                for t in range(NT):
                    dve.wait_ge(unit_used, end)
                    nc.vector.tensor_tensor(xs[:, t, :].rearrange("p (h n) -> p h n", h=2),
                                            psum[:, banks[2 * t]:banks[2 * t] + 2, :],
                                            xs[:, t, :].rearrange("p (h n) -> p h n", h=2), ALU.add).then_inc(x_added, 1)

            def head_sums(events, heads):
                for e in events:
                    dve.wait_ge(head_sq, e + 1)
                    sq = (e_sq if e < 4 else m_sq)[:, e % 2, 0:heads * HD]
                    nc.vector.tensor_reduce(head_ss[:, e, 0:heads], sq.rearrange("p (h d) -> p h d", h=heads),
                                            AX_X, ALU.add).then_inc(head_sum, 1)

            def head_scale(e, src, dst, heads):
                dve.wait_ge(head_rs_ready, e + 1)
                nc.vector.tensor_tensor(dst, src, heads, ALU.mult).then_inc(head_normed, 1)

            def softmax_max(a, h, lb):
                dve.wait_ge(logits_ready, 8 * a + h + 1)
                if h >= 2:
                    dve.wait_ge(exp_ready, 2 * (8 * a + h - 1))
                b = h % 2
                for t, (c0, c1) in enumerate(((0, P), (P, TRI))):
                    nc.vector.tensor_reduce(row_max[:, b, t:t + 1], bank(lb[b], c0, c1), AX_X, ALU.max, negate=True
                                            ).then_inc(max_ready, 1)

            def softmax_norm(a, h):
                b = h % 2
                dve.wait_ge(exp_ready, 2 * (8 * a + h) + 2)
                nc.vector.reciprocal(row_inv[:, b, :], row_sum[:, b, :]).then_inc(inv_ready, 1)
                dve.wait_ge(inv_ready, 8 * a + h + 1)
                for t, (c0, c1) in enumerate(((0, P), (P, TRI))):
                    nc.vector.tensor_scalar(probs[:, b, c0:c1], probs[:, b, c0:c1], row_inv[:, b, t:t + 1], None,
                                            ALU.mult).then_inc(probs_ready, 1)

            def softmax_out(a, j):
                dve.wait_ge(pv_high, 4 * a + j + 1)
                nc.vector.tensor_tensor(ml[:, j, :], bank(PV_BANK, 0, SEQ), mh[:, j, :].bitcast(F32), ALU.subtract
                                        ).then_inc(pv_low, 1)

            def softmax_start(a, lb):
                softmax_max(a, 0, lb)
                softmax_max(a, 1, lb)
                softmax_norm(a, 0)

            def softmax_head(a, h, lb):
                if h + 1 < 8:
                    softmax_norm(a, h + 1)
                if h + 2 < 8:
                    softmax_max(a, h + 2, lb)
                if h % 2:
                    softmax_out(a, h // 2)

            def ffn(f):
                n0 = U_FFN[f]

                def gated(c):
                    for t in range(NT):
                        dve.wait_ge(silu_ready, 2 * (FSTEPS * f + c) + t + 1)
                        if f or c_late(c):
                            dve.wait_ge(hiddenT_ready, FSTEPS * f + c)
                        nc.vector.tensor_tensor(f_hidden[:, t, :], bank(SET_A[t], FC, 2 * FC), f_silu[:, t, :], ALU.mult
                                                ).then_inc(hidden_ready, 1)

                def hiddenT(c):
                    dve.wait_ge(gh_ready, FSTEPS * f + c + 1)
                    nc.vector.tensor_tensor(gl[:], bank(6).rearrange("p (k n) -> p k n", k=2), gh[:].bitcast(F32),
                                            ALU.subtract).then_inc(gl_ready, 1)

                def step(c, i):
                    n = n0 + 2
                    split_low(n + 3, i)
                    hiddenT(c - 1)
                    gated(c)
                    split_low(n + 4, i)
                    split_low(n + 5, i)

                split_low(n0 + 3)
                gated(0)
                split_low(n0 + 4)
                step(1, 0)
                ahead = 0 if n0 + 3 * FSTEPS < N_UNITS else 1
                with dve.Fori(1, FSTEPS - 1 - ahead) as i:
                    step(i + 1, i)
                if ahead:
                    step(FSTEPS - 1, FSTEPS - 2)
                hiddenT(FSTEPS - 1)
                add_residual(n0 + 3 * FSTEPS, TALL_MID)
                split_low(n0 + 3 * FSTEPS + 2)

            normalise(0, 0, 0)
            dve.wait_ge(small_in, 16 * 10)
            nc.vector.tensor_scalar(q_gain, head_gain[:, 0:4:2], QK_SCALE, None, ALU.mult).then_inc(q_gain_ready, 1)
            for n in range(RING):
                split_low(n)
            xT_low(0, xh, xl)

            split_low(U_KI + 3)
            split_low(U_KI + 4)
            split_low(U_KI + 5)
            head_sums((0, 1), 2)
            for t in range(NT):
                dve.wait_ge(vqi_copied, t + 1)
                head_scale(t, bank(SET_B[t], 0, P).rearrange("p (h d) -> p h d", h=2),
                           e_kn[:, t, :].rearrange("p (h d) -> p h d", h=2),
                           head_rs[:, t, 0:2].unsqueeze(2).to_broadcast([P, 2, HD]))
            split_low(U_KI + 6)
            dve.wait_ge(kiT_ready, 1)
            nc.vector.tensor_copy(e_kiT, bank(4, 0, SEQ)).then_inc(kiT_copied, 1)
            dve.wait_ge(qiT_ready, 1)
            nc.vector.tensor_copy(e_qiT, bank(5).rearrange("p (j n) -> p j n", j=2)).then_inc(qiT_copied, 1)
            split_low(U_KI + 7)
            head_sums((2, 3), 8)
            split_low(U_KI + 8)
            for t in range(NT):
                head_scale(2 + t, bank(SET_A[t]).rearrange("p (g r d) -> p g r d", g=2, r=4),
                           e_qn[:, t, :].rearrange("p (r g d) -> p g r d", g=2, r=4),
                           head_rs[:, 2 + t, :].rearrange("p (g r) -> p g r", g=2).unsqueeze(3).to_broadcast([P, 2, 4, HD]))
            steps = 0

            def step(ins):
                nonlocal steps
                steps += 1
                ins.then_inc(topk_step, 1)
                dve.wait_ge(topk_step, steps)

            dve.wait_ge(idx_w_copied, 2)
            dve.wait_ge(consts_in, 16)
            for t in range(NT):
                k = (t + 1) * P
                mask = causal[:, t * P:t * P + k]
                score = e_score[:, 0:k]
                dve.wait_ge(rel_ready, t + 1)
                for h in range(IDX_HEADS):
                    step(nc.vector.scalar_tensor_tensor(out=score, in0=e_rel[:, t, h, 0:k], scalar=idx_w[:, t, h:h + 1],
                                                        in1=score if h else mask, op0=ALU.mult, op1=ALU.add))
                for _ in range(N_SEL // 8):
                    step(nc.vector.max(top8, score))
                    step(nc.vector.match_replace(score, top8, score, TAKEN))
                step(nc.vector.tensor_scalar(e_hit[:, 0:k], score, TAKEN, -MASKED, ALU.is_equal, ALU.mult))
                nc.vector.scalar_tensor_tensor(out=selbias[:, t * P:t * P + k], in0=e_hit[:, 0:k], scalar=MASKED, in1=mask,
                                               op0=ALU.add, op1=ALU.add).then_inc(sel_ready, 1)
                if t == 0:
                    split_low(U_KI + 9)
                    split_low(U_KI + 10)
                    for g in range(4):
                        dve.wait_ge(poolmix_high, 2 * (g // 2) + 2)
                        nc.vector.scalar_tensor_tensor(out=ml[:, 4 + g, :], in0=bank(2 + g // 2, (g % 2) * SEQ, (g % 2 + 1) * SEQ),
                                                       scalar=pool_gain[:, g:g + 1], in1=mh[:, 4 + g, :].bitcast(F32),
                                                       op0=ALU.mult, op1=ALU.subtract).then_inc(poolmix_low, 1)
            split_low(U_EOUT + 3)
            split_low(U_EOUT + 4)
            softmax_start(0, E_LB)
            for h in range(8):
                softmax_head(0, h, E_LB)
            split_low(U_EOUT + 5)
            add_residual(U_FFN[0], TALL_MID)
            split_low(U_EOUT + 6)
            normalise(1, 1, 1)
            xT_low(1, xh, xl)
            ffn(0)

            normalise(2, 2, 2)
            xT_low(2, xh, xl)

            def stick_brk(p):
                dve.wait_ge(log_ready, p + 1)
                if p >= 2:
                    dve.wait_ge(loga_ready, p - 1)
                b = 4 + 2 * (p % 2)
                nc.vector.scalar_tensor_tensor(out=o_brk[:, p % 2], in0=psum[:, b:b + 2, 0:TRI], scalar=0.0, in1=o_log,
                                               op0=ALU.max, op1=ALU.add).then_inc(brk_ready, 1)

            def stick_out(p):
                dve.wait_ge(sbv_high, p + 1)
                b = 4 + 2 * (p % 2)
                nc.vector.tensor_tensor(ml[:, p, :].rearrange("p (t n) -> p t n", t=NT), psum[:, b:b + 2, TRI:512],
                                        mh[:, p, :].bitcast(F32).rearrange("p (t n) -> p t n", t=NT), ALU.subtract
                                        ).then_inc(sbv_low, 1)

            def stick_slot(s, first, n):
                if s >= 2:
                    stick_out(first + s - 2)
                if s < n:
                    stick_brk(first + s)

            U = U_QKV[0]
            for half in range(2):
                for j in range(6):
                    split_low(U + 6 * half + j + 3)
                    if half == 0 and j == 5:
                        stick_slot(0, 0, 4)
                    if half == 1 and j < 5:
                        stick_slot(j + 1, 0, 4)
            split_low(U_OOUT + 3)
            stick_slot(0, 4, 4)
            split_low(U_OOUT + 4)
            for s in range(1, 4):
                stick_slot(s, 4, 4)
            split_low(U_OOUT + 5)
            stick_slot(4, 4, 4)
            stick_slot(5, 4, 4)
            add_residual(U_FFN[1], TALL_LOW)
            split_low(U_OOUT + 6)
            normalise(3, 3, 3)
            xT_low(3, xh, xl)
            ffn(1)

            normalise(4, 4, 4)
            xT_low(4, xh, xl)
            gn_steps = 0
            U = U_P2[0]
            for j in range(2 * len(U_P2)):
                c, last = divmod(j, 2)
                if last and c < 2:
                    head_sums((4 + 2 * c, 5 + 2 * c), 8)
                split_low(U + j + 3)
                if last and c < 2:
                    for t in range(NT):
                        if c == 1:
                            dve.wait_ge(headT_ready, 4 + t + 1 - 1)
                        head_scale(4 + 2 * c + t, bank((SET_A, SET_B)[c][t]).rearrange("p (h d) -> p h d", h=8),
                                   m_tok[:, t, :].rearrange("p (h d) -> p h d", h=8),
                                   head_rs[:, 4 + 2 * c + t, :].unsqueeze(2).to_broadcast([P, 8, HD]))
                if last and c in (3, 4):
                    unit = U_P2[c]
                    s = chunk_set(unit)
                    for t in range(NT):
                        chunk_done(dve, unit, t)
                        src = bank((SET_A, SET_B)[s][t]).rearrange("p (h x d) -> p h x d", h=RET_HEADS, x=2)
                        dst = r_tok[:, t, c - 3, :].rearrange("p (h x d) -> p h x d", h=RET_HEADS, x=2)
                        tmp = r_half[:, t, :].rearrange("p (h x d) -> p h x d", h=RET_HEADS, x=2)
                        table = rope[:, t].rearrange("p c (x d) -> p c x d", x=2)

                        def spread(r, x):
                            return table[:, r, x, :].unsqueeze(1).to_broadcast([P, RET_HEADS, HD])

                        for x in range(2):
                            nc.vector.tensor_tensor(dst[:, :, x, :], src[:, :, x, :], spread(0, x), ALU.mult).then_inc(rope_step, 1)
                            nc.vector.tensor_tensor(tmp[:, :, x, :], src[:, :, 1 - x, :], spread(1, x), ALU.mult).then_inc(rope_step, 1)
                        dve.wait_ge(rope_step, 4 * (2 * (c - 3) + t + 1))
                        nc.vector.tensor_tensor(r_tok[:, t, c - 3, :], r_tok[:, t, c - 3, :], r_half[:, t, :], ALU.add).then_inc(roped, 1)
                if j == 6:
                    softmax_start(1, M_LB)
                if 7 <= j < 15:
                    softmax_head(1, j - 7, M_LB)
                if j == 18:
                    dve.wait_ge(consts_in, 32)
                    for h in range(RET_HEADS):
                        dve.wait_ge(rscore_ready, h + 1)
                        nc.vector.tensor_tensor(r_a[:, h, :], bank(4 + h, 0, TRI), decay[:, h, :], ALU.mult).then_inc(decayed, 1)
                if j == 20:
                    for t in range(NT):
                        for h in range(RET_HEADS):
                            dve.wait_ge(ro_ready, h + 1)
                            nc.vector.bn_stats(gn_stats[:, t, h, :], bank(4 + h, t * RET_DV, (t + 1) * RET_DV)).then_inc(gn_done, 1)
                        for h in range(RET_HEADS):
                            dve.wait_ge(gn_done, RET_HEADS * t + h + 1)
                            ins = nc.vector.bn_aggr(gn_mv[:, t, h, :], gn_stats[:, t, h, :])
                        ins.then_inc(gn_var_ready, 1)
                if j == 22:
                    dve.wait_ge(rg_ready, 4)
                    for t in range(NT):
                        dve.wait_ge(gn_rstd_ready, t + 1)
                        for h in range(RET_HEADS):
                            s = slice(h * RET_DV, (h + 1) * RET_DV)
                            nc.vector.tensor_scalar(r_o[:, t, s], bank(4 + h, t * RET_DV, (t + 1) * RET_DV),
                                                    gn_mv[:, t, h, 0:1], gn_rstd[:, t, h:h + 1], ALU.subtract, ALU.mult
                                                    ).then_inc(ret_ready, 1)
                        dve.wait_ge(ret_ready, 5 * t + RET_HEADS)
                        nc.vector.tensor_tensor(r_o[:, t, :], r_o[:, t, :], r_gate[:, t, :], ALU.mult).then_inc(ret_ready, 1)
            split_low(U_MOBA + 3)
            split_low(U_MOBA + 4)
            for t in range(NT):
                for q in range(2):
                    dve.wait_ge(ret_high, 2 * t + q + 1)
                    s = (slice(None), slice(4 * q, 4 * q + 4), slice(t * P, (t + 1) * P))
                    nc.vector.tensor_tensor(xl[s], bank(2 + 2 * t + q).rearrange("p (k n) -> p k n", k=4),
                                            xh[s].bitcast(F32), ALU.subtract).then_inc(ret_low, 1)

            def halves(ap):
                return ap.rearrange("p (h n) -> p h n", h=2)

            dve.wait_ge(gates_ready, 8)
            for t in range(NT):
                dve.wait_ge(unit_used, U_RET)
                for h in range(2):
                    s = slice(h * 512, (h + 1) * 512)
                    nc.vector.tensor_tensor(gate_b[:, t, s], bank(TALL_ENDS[2 * t + h]), gate_b[:, t, s], ALU.mult
                                            ).then_inc(b_gated, 1)
            for n in range(U_RET, U_WO):
                split_low(n + 3)
            for t in range(NT):
                dve.wait_ge(unit_used, U_WO)
                nc.vector.tensor_tensor(halves(gate_a[:, t, :]), psum[:, 2 + 2 * t:4 + 2 * t, :], halves(gate_a[:, t, :]),
                                        ALU.mult).then_inc(a_gated, 1)
                dve.wait_ge(a_gated, t + 1)
                dve.wait_ge(b_gated, 2 * t + 2)
                dve.wait_ge(retT_ready, 4)
                nc.vector.tensor_tensor(xn[:, t, :], gate_a[:, t, :], gate_b[:, t, :], ALU.add).then_inc(xn_ready, 1)
            xT_low(5, mh, ml)
            for n in range(U_WO, U_FFN[2] - 1):
                split_low(n + 3)
            add_residual(U_FFN[2], TALL_MID)
            split_low(U_FFN[2] + 2)
            normalise(6, 5, 5)
            xT_low(6, xh, xl)
            ffn(2)

        @block.tensor
        def _(pe):
            def three_products(out, n, k, cols, sh, sl, c0, c1, start, stop):
                wh, wl = slot_tile(high, n, k, cols)[:, c0:c1], slot_tile(low, n, k, cols)[:, c0:c1]
                nc.tensor.matmul(out, sh, wh, start=start, stop=False, skip_group_check=True)
                nc.tensor.matmul(out, sh, wl, start=False, stop=False, skip_group_check=True)
                return nc.tensor.matmul(out, sl, wh, start=False, stop=stop, skip_group_check=True)

            def wide_unit(n, second, banks, cols, done, i=0, xk=None):
                pe.wait_ge(low_ready, n + 1 + 3 * i)
                for t in range(NT):
                    if xk is not None:
                        pe.wait_ge(xl_ready, 4 * xk + 2 * t + 2)
                    for k in range(4):
                        kk = 4 * second + k
                        s = (slice(None), kk, slice(t * P, (t + 1) * P))
                        ins = three_products(bank(banks[t], 0, cols), n, k, cols, xh[s], xl[s], 0, cols,
                                             kk == 0, kk == KD - 1)
                    if second and t == 0:
                        ins.then_inc(done, 1)
                ins.then_inc(unit_used, 1)

            def wide(unit, second, cols=512, xk=None):
                s = chunk_set(unit)
                if not second:
                    for q, v in reads_before(unit):
                        pe.wait_ge(q, v)
                wide_unit(unit + second, second, (SET_A, SET_B)[s], cols, wide_ready[s], xk=xk)

            def tall_unit(n, sh, sl, k0, banks, start, stop, i=0):
                pe.wait_ge(low_ready, n + 1 + 3 * i)
                for t in range(NT):
                    for k in range(2):
                        s = (slice(None), k0 + k, slice(t * P, (t + 1) * P))
                        for h in range(2):
                            ins = three_products(bank(banks[2 * t + h]), n, k, D, sh[s], sl[s], h * 512, (h + 1) * 512,
                                                 start and k == 0, stop and k == 1)
                ins.then_inc(unit_used, 1)

            def transposes(dst_bank, srcs, done):
                for j, src in enumerate(srcs):
                    ins = nc.tensor.transpose(bank(dst_bank, j * P, (j + 1) * P), src, ident)
                ins.then_inc(done, 1)

            def xT(k):
                for t in range(NT):
                    pe.wait_ge(xn_ready, 2 * k + t + 1)
                    for q in range(2):
                        transposes(XT_BANKS[t][q], [xn[:, t, (4 * q + j) * P:(4 * q + j + 1) * P] for j in range(4)], xT_ready)

            def softmax_logits(a, h, lb, qT, kT, mask):
                b = h % 2
                if h >= 2:
                    pe.wait_ge(exp_ready, 2 * (8 * a + h - 1))
                for t, (c0, c1) in enumerate(((0, P), (P, TRI))):
                    dst = bank(lb[b], c0, c1)
                    nc.tensor.matmul(dst, qT[:, t * P:(t + 1) * P], kT[:, 0:c1 - c0], start=True, stop=False, skip_group_check=True)
                    ins = nc.tensor.matmul(dst, identr[:], mask[:, c0:c1], start=False, stop=True, skip_group_check=True)
                ins.then_inc(logits_ready, 1)

            def softmax_T(a, h):
                pe.wait_ge(probs_ready, 2 * (8 * a + h) + 2)
                if h:
                    pe.wait_ge(probsT_copied, 8 * a + h)
                b = h % 2
                transposes(PT_BANK, [probs[:, b, j * P:(j + 1) * P] for j in range(3)], probsT_ready)

            def softmax_pv(a, h, v):
                b = h % 2
                pe.wait_ge(probsT_copied, 8 * a + h + 1)
                if h >= 2:
                    pe.wait_ge(pv_low, 4 * a + h // 2)
                rows = slice(b * HD, (b + 1) * HD)
                dst = [psum[rows, PV_BANK, t * P:(t + 1) * P] for t in range(NT)]
                nc.tensor.matmul(dst[0], v(0), probsT[:, b, 0:P], start=True, stop=True, skip_group_check=True)
                nc.tensor.matmul(dst[1], v(0), probsT[:, b, P:2 * P], start=True, stop=False, skip_group_check=True)
                nc.tensor.matmul(dst[1], v(1), probsT[:, b, 2 * P:TRI], start=False, stop=True, skip_group_check=True
                                 ).then_inc(pv_ready, 1)

            def ffn(f, xk):
                n0 = U_FFN[f]

                def hiddenT(c):
                    pe.wait_ge(hidden_ready, 2 * (FSTEPS * f + c) + 2)
                    if f or c_late(c):
                        pe.wait_ge(gl_ready, FSTEPS * f + c)
                    transposes(6, [f_hidden[:, t, k * P:(k + 1) * P] for k in range(2) for t in range(NT)], hiddenT_ready)

                def down(n, c, start, stop, i=0):
                    pe.wait_ge(gl_ready, FSTEPS * f + c + 1)
                    tall_unit(n, gh, gl, 0, TALL_MID, start, stop, i)

                def step(c, i, start):
                    n = n0 + 2
                    pe.wait_ge(hidden_ready, 2 * (FSTEPS * f + c))
                    wide_unit(n, 0, SET_A, 512, wide_ready[0], i)
                    hiddenT(c - 1)
                    wide_unit(n + 1, 1, SET_A, 512, wide_ready[0], i)
                    down(n + 2, c - 1, start, False, i)

                wide_unit(n0, 0, SET_A, 512, wide_ready[0], xk=xk)
                wide_unit(n0 + 1, 1, SET_A, 512, wide_ready[0])
                step(1, 0, True)
                with pe.Fori(1, FSTEPS - 1) as i:
                    step(i + 1, i, False)
                hiddenT(FSTEPS - 1)
                down(n0 + 3 * FSTEPS - 1, FSTEPS - 1, False, True)

            pe.wait_ge(consts_in, 16)
            xT(0)
            wide(U_KI, 0, KI_COLS, xk=0)
            wide(U_KI, 1, KI_COLS)
            wide(U_KVQI, 0)
            wide(U_KVQI, 1)
            wide(U_Q, 0)
            pe.wait_ge(ki_copied, 2)
            transposes(4, [e_kk[:, t, :] for t in range(NT)], kiT_ready)
            pe.wait_ge(vqi_copied, 2)
            transposes(5, [e_vqi[:, t, P + j * P:P + (j + 1) * P] for j in range(2) for t in range(NT)], qiT_ready)
            pe.wait_ge(head_normed, 2)
            transposes(6, [e_kn[:, t, :] for t in range(NT)], headT_ready)
            wide(U_Q, 1)
            pe.wait_ge(kiT_copied, 1)
            pe.wait_ge(qiT_copied, 1)
            pe.wait_ge(headT_copied, 1)
            for t in range(NT):
                k = (t + 1) * P
                for h in range(IDX_HEADS):
                    rows = slice((h % 2) * HD, (h % 2 + 1) * HD)
                    ins = nc.tensor.matmul(bank(4 + 2 * t + h % 2, (h // 2) * k, (h // 2 + 1) * k),
                                           e_qiT[rows, h // 2, t * P:(t + 1) * P], e_kiT[rows, 0:k], start=True, stop=True,
                                           skip_group_check=True)
                ins.then_inc(idx_ready, 1)
            wide(U_POOL, 0)
            for t in range(NT):
                pe.wait_ge(head_normed, 3 + t)
                pe.wait_ge(rel_ready, 1)
                transposes(4 + t, [e_qn[:, t, j * P:(j + 1) * P] for j in range(4)], headT_ready)
            wide(U_POOL, 1)
            pe.wait_ge(u_copied, 2)
            for g in range(4):
                dst = bank(g // 2, (g % 2) * SEQ, (g % 2 + 1) * SEQ)
                c = slice(g * P, (g + 1) * P)
                nc.tensor.matmul(dst, e_u[:, 0, c], bands[:, g, 0:SEQ], start=True, stop=False, skip_group_check=True)
                ins = nc.tensor.matmul(dst[:, P:SEQ], e_u[:, 1, c], bands[:, g, SEQ:TRI], start=False, stop=True,
                                       skip_group_check=True)
            ins.then_inc(pooled_ready, 1)
            pe.wait_ge(pooled_copied, 1)
            pe.wait_ge(small_in, 16 * 10)
            for g in range(4):
                ins = nc.tensor.matmul(bank(2 + g // 2, (g % 2) * SEQ, (g % 2 + 1) * SEQ), poolw[:, g, :], e_pm[:, g, :],
                                       start=True, stop=True, skip_group_check=True)
            ins.then_inc(poolmix_ready, 1)

            def even_logits(h):
                g, r = divmod(h, 4)
                rows = slice(g * HD, (g + 1) * HD)
                softmax_logits(0, h, E_LB, e_qT[rows, r, :], e_kT[rows, :], selbias)

            pe.wait_ge(poolmix_low, 4)
            tall_unit(U_EOUT, mh, ml, 4, TALL_MID, True, False)
            tall_unit(U_EOUT + 1, mh, ml, 6, TALL_MID, False, False)
            pe.wait_ge(masks_ready, 3)
            pe.wait_ge(headT_copied, 3)
            pe.wait_ge(sel_ready, 2)
            even_logits(0)
            even_logits(1)
            for h in range(8):
                softmax_T(0, h)
                if h + 2 < 8:
                    even_logits(h + 2)
                softmax_pv(0, h, lambda b: e_vqi[:, b, (h // 4) * HD:(h // 4 + 1) * HD])
            for j in range(2):
                pe.wait_ge(pv_low, 2 * j + 2)
                tall_unit(U_EOUT + 2 + j, mh, ml, 2 * j, TALL_MID, False, j == 1)
            xT(1)
            ffn(0, 1)

            xT(2)

            def qk_T(half, f):
                for t in range(NT):
                    pe.wait_ge(qkv_copied, 4 * half + 2 * f + t + 1)
                    transposes(4 + 2 * f + t, [o_tok[:, f, t, j * P:(j + 1) * P] for j in range(4)], qkvT_ready)

            def stick_z(p):
                half, j = divmod(p, 4)
                if j == 0:
                    pe.wait_ge(qkvT_copied, 4 * half + 4)
                if p >= 2:
                    pe.wait_ge(sbv_low, p - 1)
                for e in range(2):
                    b = 4 + 2 * (p % 2) + e
                    rows = slice(e * HD, (e + 1) * HD)
                    q, k = o_qT[rows, half, j, :], o_kT[rows, half, j, :]
                    nc.tensor.matmul(bank(b, 0, SEQ), k[:, 0:P], q, start=True, stop=False, skip_group_check=True)
                    nc.tensor.matmul(bank(b, SEQ, TRI), k[:, P:SEQ], q[:, P:SEQ], start=False, stop=False, skip_group_check=True)
                    nc.tensor.matmul(bank(b, 0, P), identr[:], strictr[:], start=False, stop=False, skip_group_check=True)
                    ins = nc.tensor.matmul(bank(b, SEQ, TRI), identr[:], strictr[:], start=False, stop=True, skip_group_check=True)
                ins.then_inc(z_ready, 1)

            def stick_remain(p):
                pe.wait_ge(brk_ready, p + 1)
                for e in range(2):
                    b = 4 + 2 * (p % 2) + e
                    brk = o_brk[:, p % 2, e, :]
                    nc.tensor.matmul(bank(b, 0, SEQ), tri_neg, brk[:, 0:SEQ], start=False, stop=False, skip_group_check=True)
                    nc.tensor.matmul(bank(b, P, SEQ), ones_neg, brk[:, SEQ:TRI], start=False, stop=False, skip_group_check=True)
                    ins = nc.tensor.matmul(bank(b, SEQ, TRI), tri_neg, brk[:, SEQ:TRI], start=False, stop=True, skip_group_check=True)
                ins.then_inc(loga_ready, 1)

            def stick_pv(p):
                half, j = divmod(p, 4)
                pe.wait_ge(a_ready, p + 1)
                if j == 0:
                    pe.wait_ge(v_copied, 2 * half + 2)
                for e in range(2):
                    a = o_a[:, p % 2, e, :]
                    v = [o_v[:, half, b, (2 * j + e) * HD:(2 * j + e + 1) * HD] for b in range(NT)]
                    dst = [psum[e * HD:(e + 1) * HD, 4 + 2 * (p % 2) + t, TRI:512] for t in range(NT)]
                    nc.tensor.matmul(dst[0], v[0], a[:, 0:P], start=True, stop=True, skip_group_check=True)
                    nc.tensor.matmul(dst[1], v[0], a[:, P:SEQ], start=True, stop=False, skip_group_check=True)
                    ins = nc.tensor.matmul(dst[1], v[1], a[:, SEQ:TRI], start=False, stop=True, skip_group_check=True)
                ins.then_inc(sbv_ready, 1)

            def stick_slot(s, first, n):
                if s >= 2:
                    stick_pv(first + s - 2)
                if 1 <= s <= n:
                    stick_remain(first + s - 1)
                if s < n:
                    stick_z(first + s)

            for half in range(2):
                for j in range(6):
                    f, second = divmod(j, 2)
                    wide(U_QKV[3 * half + f], second, xk=2 if j == 0 and half == 0 else None)
                    if half == 0:
                        if j == 2:
                            qk_T(0, 0)
                        if j == 4:
                            qk_T(0, 1)
                        if j == 5:
                            stick_slot(0, 0, 4)
                    else:
                        if j < 5:
                            stick_slot(j + 1, 0, 4)
                        if j == 4:
                            pe.wait_ge(sbv_low, 4)
                            qk_T(1, 0)
                        if j == 5:
                            qk_T(1, 1)
            for q, v in reads_before(U_P2[0]) + [(v_copied, 4)]:
                pe.wait_ge(q, v)
            tall_unit(U_OOUT, mh, ml, 0, TALL_LOW, True, False)
            stick_slot(0, 4, 4)
            tall_unit(U_OOUT + 1, mh, ml, 2, TALL_LOW, False, False)
            for s in range(1, 4):
                stick_slot(s, 4, 4)
            stick_slot(4, 4, 4)
            tall_unit(U_OOUT + 2, mh, ml, 4, TALL_LOW, False, False)
            stick_slot(5, 4, 4)
            pe.wait_ge(sbv_low, 8)
            tall_unit(U_OOUT + 3, mh, ml, 6, TALL_LOW, False, True)
            xT(3)
            ffn(1, 3)

            xT(4)

            def moba_logits(h):
                rows = slice((h % 2) * HD, (h % 2 + 1) * HD)
                softmax_logits(1, h, M_LB, m_qT[rows, h // 2, :], m_kT[rows, h // 2, :], causalr)

            for j in range(2 * len(U_P2)):
                c, second = divmod(j, 2)
                wide(U_P2[c], second, xk=4 if j == 0 else None)
                if j in (3, 5):
                    f = (j - 3) // 2
                    for t in range(NT):
                        pe.wait_ge(head_normed, 4 + 2 * f + t + 1)
                        transposes(4 + 2 * f + t, [m_tok[:, t, i * P:(i + 1) * P] for i in range(4)], headT_ready)
                if j == 6:
                    pe.wait_ge(headT_copied, 7)
                    moba_logits(0)
                    moba_logits(1)
                    pe.wait_ge(mv_copied, 2)
                if 7 <= j < 15:
                    h = j - 7
                    softmax_T(1, h)
                    if h + 2 < 8:
                        moba_logits(h + 2)
                    softmax_pv(1, h, lambda b: m_v[:, b, h * HD:(h + 1) * HD])
                if j in (16, 17):
                    f = j - 16
                    pe.wait_ge(pv_low, 8)
                    for t in range(NT):
                        pe.wait_ge(roped, 2 * f + t + 1)
                        transposes(4 + 2 * f + t, [r_tok[:, t, f, i * P:(i + 1) * P] for i in range(4)], ropeT_ready)
                if j == 18:
                    pe.wait_ge(ropeT_copied, 4)
                    for h in range(RET_HEADS):
                        nc.tensor.matmul(bank(4 + h, 0, SEQ), r_kT[:, h, 0:P], r_qT[:, h, :], start=True, stop=True, skip_group_check=True)
                        nc.tensor.matmul(bank(4 + h, SEQ, TRI), r_kT[:, h, P:SEQ], r_qT[:, h, P:SEQ], start=True, stop=True,
                                         skip_group_check=True).then_inc(rscore_ready, 1)
                if j == 20:
                    pe.wait_ge(rv_copied, 4)
                    for h in range(RET_HEADS):
                        pe.wait_ge(decayed, h + 1)
                        v = [r_v[:, b, h * RET_DV:(h + 1) * RET_DV] for b in range(NT)]
                        nc.tensor.matmul(bank(4 + h, 0, RET_DV), r_a[:, h, 0:P], v[0], start=True, stop=True, skip_group_check=True)
                        nc.tensor.matmul(bank(4 + h, RET_DV, 512), r_a[:, h, P:SEQ], v[0], start=True, stop=False, skip_group_check=True)
                        nc.tensor.matmul(bank(4 + h, RET_DV, 512), r_a[:, h, SEQ:TRI], v[1], start=False, stop=True,
                                         skip_group_check=True).then_inc(ro_ready, 1)
            pe.wait_ge(gates_ready, 8)
            pe.wait_ge(ret_ready, 5 * NT)
            for p in range(2):
                tall_unit(U_MOBA + p, mh, ml, 2 * p, TALL_ENDS, p == 0, p == 1)
            for t in range(NT):
                for q in range(2):
                    transposes(2 + 2 * t + q, [r_o[:, t, (4 * q + i) * P:(4 * q + i + 1) * P] for i in range(4)], retT_ready)
            pe.wait_ge(ret_low, 4)
            for p in range(4):
                tall_unit(U_RET + p, xh, xl, 2 * p, TALL_MID, p == 0, p == 3)
            pe.wait_ge(b_gated, 4)
            xT(5)
            pe.wait_ge(xl_ready, 4 * 6)
            for p in range(4):
                tall_unit(U_WO + p, mh, ml, 2 * p, TALL_MID, p == 0, p == 3)
            xT(6)
            ffn(2, 6)


_INS = ['x', 'norm_mix_g', 'norm_ffn_g', 'ev_w_in', 'ev_w_out', 'ev_q_norm_g', 'ev_k_norm_g', 'ev_pool_w',
        'ev_pool_scale', 'od_w_qkv', 'od_w_out', 'ffn_w1', 'ffn_w3', 'ffn_w2', 'norm1_w_2', 'w_in_2', 'q_norm_w_2',
        'k_norm_w_2', 'w_ret_out_2', 'w_moba_out_2', 'w_o_2', 'norm2_w_2', 'w_ffn_gate_2', 'w_ffn_up_2',
        'w_ffn_down_2']


def kernel(**inputs):
    import concourse.bacc as bacc
    from concourse.bass_utils import run_bass_kernel_spmd

    nc = bacc.Bacc("TRN2", target_bir_lowering=False, num_devices=1)
    arrays, args = {}, []
    for name in _INS:
        a = np.ascontiguousarray(inputs[name])
        arrays[f"in_{name}"] = a
        args.append(nc.dram_tensor(f"in_{name}", a.shape, mybir.dt.from_np(a.dtype), kind="ExternalInput").ap())
    arrays["consts"] = constants()
    args.append(nc.dram_tensor("consts", (P, CONST_N), F32, kind="ExternalInput").ap())
    args.append(nc.dram_tensor("out", (1, SEQ, D), F32, kind="ExternalOutput").ap())
    program(nc, *args)
    r = run_bass_kernel_spmd(nc, [arrays], core_ids=[0])
    return r.results[0]["out"]
```

```python
from contextlib import ExitStack

import concourse.bass as bass
from concourse import mybir
import numpy as np

F32 = mybir.dt.float32
F32R = mybir.dt.float32r
ALU = mybir.AluOpType
ACT = mybir.ActivationFunctionType
AX_X = mybir.AxisListType.X

P = 128
SEQ = 256
NT = SEQ // P
D = 1024
KD = D // P
HD = 64
FF = 2816
FC = 256
FSTEPS = FF // FC
EPS = 1e-6
GN_EPS = 1e-5
N_SEL = 64
IDX_HEADS = 4
IDX_SCALE = (IDX_HEADS * HD) ** -0.5
QK_SCALE = HD ** -0.5
RET_HEADS = 4
RET_DV = 256
RET_SCALE = 128 ** -0.5
MASKED = -(2.0 ** 100)
TAKEN = -(2.0 ** 127)
TRI = P + SEQ
UNIT = 2048
RING = 3
SETS = SET_A, SET_B, SET_C = (0, 1), (2, 3), (4, 5)
TALL_MID, TALL_LOW = (2, 3, 4, 5), (0, 1, 2, 3)
TALL_ENDS, TALL_SPLIT = (6, 7, 0, 1), (0, 1, 4, 5)
XT_BANKS = ((6, 7), (2, 3))
E_LB, M_LB = (0, 1), (4, 5)
PT_BANK, PV_BANK = 6, 7

CONST_COLS = {}
_at = 0
for _name, _n in (("ident", P), ("causal", TRI), ("strict", P),
                  ("rope", NT * 2 * P), ("bands", 4 * TRI), ("decay", RET_HEADS * TRI)):
    CONST_COLS[_name] = (_at, _n)
    _at += _n
CONST_N = _at


def constants():
    c = np.zeros((P, CONST_N), np.float32)

    def put(name, a):
        at, n = CONST_COLS[name]
        c[:, at:at + n] = np.asarray(a, np.float32).reshape(P, n)

    i = np.arange(P)
    put("ident", np.eye(P))
    causal = np.where(i[None, :] <= i[:, None], 0.0, MASKED)
    put("causal", np.concatenate([causal, np.zeros((P, P)), causal], 1))
    put("strict", np.where(i[None, :] < i[:, None], 0.0, MASKED))
    t = np.arange(SEQ)
    src, dst = t[:, None], t[None, :]
    bands = []
    for w in (2, 4, 8, 16):
        full = np.where((dst >= src) & (dst - src < w), 1.0 / np.minimum(dst + 1, w), 0.0) - np.eye(SEQ)
        bands.append(np.concatenate([full[:P], full[P:, P:]], 1))
    put("bands", np.stack(bands, 1))
    lg = np.log1p(-np.exp2(-5.0 - np.arange(RET_HEADS)))
    decay = []
    for h in range(RET_HEADS):
        full = np.where(dst >= src, np.exp(np.maximum(dst - src, 0) * lg[h]), 0.0)
        decay.append(np.concatenate([full[:P], full[P:, P:]], 1))
    put("decay", np.stack(decay, 1))
    inv = np.float32(10000.0) ** (-np.arange(HD, dtype=np.float32) / np.float32(HD))
    ang = (t.astype(np.float32)[:, None] * inv[None, :]).astype(np.float32).reshape(NT, P, HD)
    cos, sin = np.cos(ang), np.sin(ang)
    rope = np.stack([np.concatenate([cos, cos], 2), np.concatenate([-sin, sin], 2)], 1)
    put("rope", rope.transpose(2, 0, 1, 3))
    return c


def program(nc, x, norm_mix_g, norm_ffn_g, ev_w_in, ev_w_out, ev_q_norm_g, ev_k_norm_g, ev_pool_w,
            ev_pool_scale, od_w_qkv, od_w_out, ffn_w1, ffn_w3, ffn_w2, norm1_w_2, w_in_2, q_norm_w_2,
            k_norm_w_2, w_ret_out_2, w_moba_out_2, w_o_2, norm2_w_2, w_ffn_gate_2, w_ffn_up_2,
            w_ffn_down_2, consts, out):
    def wide_src(w, c0, n, k0):
        return [(2 * j, n, w[(k0 + 2 * j) * P:(k0 + 2 * j + 2) * P, c0:c0 + n]) for j in range(2)]

    units = []

    def add_wide(w, c0, n=512):
        at = len(units)
        units.extend([wide_src(w, c0, n, 0), wide_src(w, c0, n, 4)])
        return at

    def add_tall(w, pairs):
        at = len(units)
        for p in pairs:
            units.append([(j, D, w[(2 * p + j) * P:(2 * p + j + 1) * P, :]) for j in range(2)])
        return at

    def add_ffn():
        at = len(units)
        units.extend([None] * (3 * FSTEPS))
        return at

    w0 = ev_w_in[0]
    KI_COLS = HD + IDX_HEADS
    U_KVQI = add_wide(w0, 512)
    U_KI = add_wide(w0, 1024, KI_COLS)
    U_POOL = add_wide(w0, 1024 + KI_COLS)
    U_Q = add_wide(w0, 0)
    U_EOUT = add_tall(ev_w_out[0], (2, 3, 0, 1))
    U_FFN = [add_ffn()]
    U_QKV = [add_wide(od_w_qkv[0], 1024 * part + 512 * half)
             for part, half in ((0, 0), (1, 0), (0, 1), (1, 1), (2, 0), (2, 1))]
    U_OOUT = add_tall(od_w_out[0], range(4))
    U_FFN.append(add_ffn())
    W2 = w_in_2[0]
    P2_COLS = (3072, 3584, 4096, 0, 512, 1024, 1536, 2048, 2560, 4608, 5120, 5632, 6144)
    U_P2 = [add_wide(W2, c) for c in P2_COLS]
    U_MOBA = add_tall(w_moba_out_2[0], range(2))
    U_RET = add_tall(w_ret_out_2[0], range(4))
    U_WO = add_tall(w_o_2[0], range(4))
    U_FFN.append(add_ffn())
    N_UNITS = len(units)
    FFN_W = [(ffn_w1[0], ffn_w3[0], ffn_w2[0]), (ffn_w1[1], ffn_w3[1], ffn_w2[1]),
             (w_ffn_gate_2[0], w_ffn_up_2[0], w_ffn_down_2[0])]
    NORM_G = [norm_mix_g[0], norm_ffn_g[0], norm_mix_g[1], norm_ffn_g[1], norm1_w_2[0], None, norm2_w_2[0]]
    NORMS = [k for k in range(7) if NORM_G[k] is not None]
    FFN_NORM = (1, 3, 6)

    with ExitStack() as ctx:
        def sb(name, shape, dt=F32):
            return ctx.enter_context(nc.sbuf_tensor(name, shape, dt))

        def sem(name):
            return ctx.enter_context(nc.semaphore(name))

        raw = sb("raw", [P, RING, UNIT])
        high = sb("high", [P, RING, UNIT], F32R)
        low = sb("low", [P, RING, UNIT], F32R)
        xs = sb("xs", [P, NT, D])
        xn = sb("xn", [P, NT, D])
        xh = sb("xh", [P, KD, SEQ], F32R)
        xl = sb("xl", [P, KD, SEQ], F32R)
        mh = sb("mh", [P, KD, SEQ], F32R)
        ml = sb("ml", [P, KD, SEQ], F32R)
        gains = sb("gains", [P, D])
        gh = sb("gh", [P, 2, SEQ], F32R)
        gl = sb("gl", [P, 2, SEQ], F32R)
        arena = sb("arena", [P, 14 * 1024])
        DECAY_AT = CONST_COLS["decay"][0]
        cst = sb("cst", [P, DECAY_AT])
        identr = sb("identr", [P, P], F32R)
        causalr = sb("causalr", [P, TRI], F32R)
        strictr = sb("strictr", [P, P], F32R)
        selbias = sb("selbias", [P, TRI], F32R)
        poolw = sb("poolw", [P, 4, P])
        small = sb("small", [P, 256])
        psum = ctx.enter_context(nc.psum_tensor("psum", [P, 8, 512], F32))

        def const(name):
            at, n = CONST_COLS[name]
            return cst[:, at:at + n]

        ident = const("ident")
        causal = const("causal")
        bands = const("bands").rearrange("p (g n) -> p g n", g=4)
        decay = bands
        rope = const("rope").rearrange("p (t c d) -> p t c d", t=NT, c=2)

        sumsq = small[:, 0:14]
        msq = small[:, 14:28]
        rstd = small[:, 28:42]
        head_ss = small[:, 48:112].rearrange("p (e h) -> p e h", h=8)
        head_ms = small[:, 112:176].rearrange("p (e h) -> p e h", h=8)
        neg_half = small[:, 176:184]
        head_gain = small[:, 184:188]
        q_gain = small[:, 188:190]
        pool_gain = small[:, 190:194]
        row_max = small[:, 194:198].rearrange("p (b t) -> p b t", t=NT)
        row_sum = small[:, 198:202].rearrange("p (b t) -> p b t", t=NT)
        row_inv = small[:, 202:206].rearrange("p (b t) -> p b t", t=NT)
        top8 = small[:, 206:214]
        idx_w = small[:, 214:222].rearrange("p (t h) -> p t h", t=NT)
        gn_mv = small[:, 222:238].rearrange("p (t h s) -> p t h s", t=NT, h=RET_HEADS)
        gn_rstd = small[:, 238:246].rearrange("p (t h) -> p t h", t=NT)
        gn_var = small[:, 246:254].rearrange("p (t h) -> p t h", t=NT)
        head_rs = sb("head_rs", [P, 8, 8])
        gn_stats = sb("gn_stats", [P, NT, RET_HEADS, 6])

        junk = arena[:, 13 * 1024:14 * 1024]
        TALLS = {u: i + 1 for i, u in enumerate((U_EOUT, U_FFN[0], U_OOUT, U_FFN[1], U_MOBA, U_RET, U_WO, U_FFN[2]))}

        def x_rstd(k, t):
            return rstd[:, 2 * k + t:2 * k + t + 1]

        class Carve:
            def __init__(self, at=0):
                self.at = at

            def __call__(self, n):
                self.at += n
                assert self.at <= 14 * 1024, self.at
                return arena[:, self.at - n:self.at]

        def blocks(ap, n):
            return ap.rearrange("p (t n) -> p t n", t=n)

        take = Carve()
        f_silu, f_hidden = blocks(take(NT * FC), NT), blocks(take(NT * FC), NT)
        take = Carve()
        probs, probsT = blocks(take(2 * TRI), 2), blocks(take(2 * TRI), 2)
        SOFTMAX_END = take.at
        e_sq = blocks(take(NT * 512), NT)
        e_kk = blocks(take(NT * P), NT)
        e_vqi = blocks(take(NT * 384), NT)
        e_kn = blocks(take(NT * P), NT)
        e_qn = blocks(take(NT * 512), NT)
        e_kiT = take(SEQ)
        e_kT = take(SEQ)
        e_qiT = blocks(take(2 * SEQ), 2)
        e_qT = blocks(take(4 * SEQ), 4)
        e_u = blocks(take(NT * 512), NT)
        e_pm = blocks(take(4 * SEQ), 4)
        e_rel = take(NT * 4 * SEQ).rearrange("p (t h k) -> p t h k", t=NT, h=IDX_HEADS)
        e_score = take(SEQ)
        e_hit = take(SEQ)
        take = Carve()
        o_tok = take(4 * 512).rearrange("p (b t n) -> p b t n", b=2, t=NT)
        o_qT = take(8 * SEQ).rearrange("p (f j t) -> p f j t", f=2, j=4)
        o_kT = take(8 * SEQ).rearrange("p (f j t) -> p f j t", f=2, j=4)
        o_v = take(4 * 512).rearrange("p (f t n) -> p f t n", f=2, t=NT)
        o_stay = take(2 * TRI).rearrange("p (e n) -> p e n", e=2)
        o_beta = take(2 * TRI).rearrange("p (e n) -> p e n", e=2)
        o_later = take(2 * TRI).rearrange("p (e n) -> p e n", e=2)
        o_a = take(2 * TRI).rearrange("p (e n) -> p e n", e=2)
        A_RING = 4
        o_aT = take(A_RING * 2 * TRI).rearrange("p (b e n) -> p b e n", b=A_RING, e=2)
        take = Carve(SOFTMAX_END)
        m_sq = blocks(take(NT * 512), NT)
        m_tok = blocks(take(NT * 512), NT)
        gate_a = blocks(take(NT * D), NT)
        m_qT = gate_a[:, 0, :].rearrange("p (j t) -> p j t", j=4)
        m_kT = gate_a[:, 1, :].rearrange("p (j t) -> p j t", j=4)
        m_v = blocks(take(NT * 512), NT)
        gate_b = blocks(take(NT * D), NT)
        r_qT = gate_b[:, 0, :].rearrange("p (j t) -> p j t", j=4)
        r_kT = gate_b[:, 1, :].rearrange("p (j t) -> p j t", j=4)
        r_v = blocks(take(NT * D), NT)
        r_gate = blocks(take(NT * D), NT)
        r_tok = xn[:, :, :].rearrange("p t (b n) -> p b t n", b=2)
        r_half = m_sq
        r_a = blocks(take(RET_HEADS * TRI), RET_HEADS)
        r_o = xn

        ident_in, consts_in, decay_in = sem("ident_in"), sem("consts_in"), sem("decay_in")
        x_in = [sem(f"x_in{t}") for t in range(NT)]
        first_gain_in, gains_in = sem("first_gain_in"), sem("gains_in")
        small_in = sem("small_in")
        landed = [sem(f"landed{i}") for i in range(RING)]
        high_ready, low_ready, unit_used = sem("high_ready"), sem("low_ready"), sem("unit_used")
        masks_ready = sem("masks_ready")
        half_ready = sem("half_ready")
        q_gain_ready = sem("q_gain_ready")
        sumsq_ready, msq_ready, rstd_ready = sem("sumsq_ready"), sem("msq_ready"), sem("rstd_ready")
        xn_ready, xT_ready, xh_ready, xl_ready = sem("xn_ready"), sem("xT_ready"), sem("xh_ready"), sem("xl_ready")
        x_added = sem("x_added")
        wide_ready = [sem("wide_ready_a"), sem("wide_ready_b"), sem("wide_ready_c")]
        tall_first = sem("tall_first")
        silu_ready, hidden_ready = sem("silu_ready"), sem("hidden_ready")
        hiddenT_ready, gh_ready, gl_ready = sem("hiddenT_ready"), sem("gh_ready"), sem("gl_ready")
        head_sq, head_sum, head_ms_ready = sem("head_sq"), sem("head_sum"), sem("head_ms_ready")
        head_pow_ready, head_rs_ready, head_normed = sem("head_pow_ready"), sem("head_rs_ready"), sem("head_normed")
        headT_ready, headT_copied = sem("headT_ready"), sem("headT_copied")
        ki_copied, vqi_copied, idx_w_copied = sem("ki_copied"), sem("vqi_copied"), sem("idx_w_copied")
        kiT_ready, qiT_ready, kiT_copied, qiT_copied = sem("kiT_ready"), sem("qiT_ready"), sem("kiT_copied"), sem("qiT_copied")
        idx_ready, rel_ready, topk_step, sel_ready = sem("idx_ready"), sem("rel_ready"), sem("topk_step"), sem("sel_ready")
        u_copied, pooled_ready, pooled_copied = sem("u_copied"), sem("pooled_ready"), sem("pooled_copied")
        poolmix_ready, poolmix_high, poolmix_low = sem("poolmix_ready"), sem("poolmix_high"), sem("poolmix_low")
        logits_ready, max_ready, exp_ready, inv_ready = sem("logits_ready"), sem("max_ready"), sem("exp_ready"), sem("inv_ready")
        probs_ready, probsT_ready, probsT_copied = sem("probs_ready"), sem("probsT_ready"), sem("probsT_copied")
        pv_ready, pv_high, pv_low = sem("pv_ready"), sem("pv_high"), sem("pv_low")
        qkv_copied, qkvT_ready, qkvT_copied, v_copied = sem("qkv_copied"), sem("qkvT_ready"), sem("qkvT_copied"), sem("v_copied")
        z_ready, stay_ready, beta_ready, ones_set = sem("z_ready"), sem("stay_ready"), sem("beta_ready"), sem("ones_set")
        later_ready, a_ready, aT_ready, aT_copied = sem("later_ready"), sem("a_ready"), sem("aT_ready"), sem("aT_copied")
        sbv_ready, sbv_high, sbv_low = sem("sbv_ready"), sem("sbv_high"), sem("sbv_low")
        mv_copied, rv_copied, rg_ready = sem("mv_copied"), sem("rv_copied"), sem("rg_ready")
        gates_ready = sem("gates_ready")
        rope_step, roped = sem("rope_step"), sem("roped")
        ropeT_ready, ropeT_copied = sem("ropeT_ready"), sem("ropeT_copied")
        rscore_ready, decayed, ro_ready = sem("rscore_ready"), sem("decayed"), sem("ro_ready")
        gn_step, gn_var_ready, gn_rstd_ready, gn_done = sem("gn_step"), sem("gn_var_ready"), sem("gn_rstd_ready"), sem("gn_done")
        ret_ready, retT_ready, ret_high, ret_low = sem("ret_ready"), sem("retT_ready"), sem("ret_high"), sem("ret_low")
        b_gated, a_gated = sem("b_gated"), sem("a_gated")
        stored = sem("stored")

        def bank(b, c0=0, c1=512):
            return psum[:, b, c0:c1]

        def slot_tile(ring, n, k, cols):
            return ring[:, n % RING, k * cols:(k + 1) * cols]

        wide_chunks = [(U_KVQI, 0, [(vqi_copied, 2), (head_normed, 2)]), (U_KI, 2, [(idx_w_copied, 2)]),
                       (U_POOL, 1, [(u_copied, 2)]), (U_Q, 0, [(head_normed, 4)])]
        wide_chunks += [(u, c % 2, [(qkv_copied, 2 * c + 2) if c < 4 else (v_copied, 2 * (c - 4) + 2)])
                        for c, u in enumerate(U_QKV)]
        P2_READS = [(head_normed, 6), (head_normed, 8), (mv_copied, 2), (roped, 2), (roped, 4), (rv_copied, 2),
                    (rv_copied, 4), (rg_ready, 2), (rg_ready, 4), (gates_ready, 2), (gates_ready, 4),
                    (gates_ready, 6), (gates_ready, 8)]
        wide_chunks += [(u, c % 2, [P2_READS[c]]) for c, u in enumerate(U_P2)]

        def reads_before(unit):
            s = chunk_set(unit)
            earlier = [reads for u, ss, reads in wide_chunks if ss == s and u < unit]
            return earlier[-1] if earlier else []

        def chunk_set(unit):
            return next(s for u, s, _ in wide_chunks if u == unit)

        def chunk_done(eng, unit, t):
            if t:
                eng.wait_ge(unit_used, unit + 2)
            else:
                s = chunk_set(unit)
                before = sum(1 for u, ss, _ in wide_chunks if ss == s and u < unit)
                steps = (FSTEPS - 1) * sum(1 for u in U_FFN if u < unit) if s == 0 else 0
                eng.wait_ge(wide_ready[s], before + steps + 1)

        def step_done(eng, f, c, t):
            if t:
                eng.wait_ge(unit_used, U_FFN[f] + (3 * c + 1 if c_late(c) else 2))
            else:
                ss = step_set(c)
                before = sum(1 for u, s, _ in wide_chunks if s == ss and u < U_FFN[f])
                eng.wait_ge(wide_ready[ss], before + ((FSTEPS - 1) * f + c if c_late(c) else f + 1))

        def step_set(c):
            return 0 if c_late(c) else 2

        def hidden_tile(first, last, c):
            return last[:, 0:2, :] if isinstance(c, int) and c == FSTEPS - 1 else first[:]

        def c_late(c):
            return not isinstance(c, int) or c > 0

        QK_T_BEFORE = {3: (0, 0), 5: (0, 1)}
        QK_T_MID = {7: (1, 0), 9: (1, 1)}
        QK_T_BANK = {(0, 0): 4, (0, 1): 6, (1, 0): 6, (1, 1): 6}
        Z_BEFORE = {6 + p: p for p in range(8)}
        A_T_BEFORE = {7 + p: p for p in range(8)}
        PV_MID = {10: (0, 1), 11: (2, 3), 12: (4, 5), 13: (6,), 14: (7,)}
        Z_BANK, A_T_BANK = 4, 6

        def pv_bank(p):
            return (A_T_BANK, Z_BANK)[p % 2]

        block = ctx.enter_context(nc.Block())

        @block.sync
        def _(sp):
            def load(n):
                if n >= RING:
                    sp.wait_ge(low_ready, n - RING + 1)
                for k0, cols, src in units[n]:
                    rows = src.shape[0] // P
                    dst = raw[:, n % RING, k0 * cols:(k0 + rows) * cols].rearrange("p (k c) -> p k c", k=rows)
                    sp.dma_start(dst, src.rearrange("(k p) c -> p k c", p=P)).then_inc(landed[n % RING], 16)

            def load_up(f, n, c, k0, after):
                sp.wait_ge(low_ready, after)
                dst = raw[:, n % RING, :].rearrange("p (k c) -> p k c", k=4)
                for j in range(2):
                    src = FFN_W[f][j][k0 * P:(k0 + 4) * P, bass.ds(c * FC, FC)]
                    sp.dma_start(dst[:, :, j * FC:(j + 1) * FC], src.rearrange("(k p) c -> p k c", p=P)
                                 ).then_inc(landed[n % RING], 16)

            def load_down(f, n, c, after):
                sp.wait_ge(low_ready, after)
                for j in range(2):
                    sp.dma_start(raw[:, n % RING, j * D:(j + 1) * D], FFN_W[f][2][bass.ds(c * FC + j * P, P), :]
                                 ).then_inc(landed[n % RING], 16)

            def load_ffn(f):
                n0 = U_FFN[f]
                load_up(f, n0, 0, 0, n0 - RING + 1)
                load_up(f, n0 + 1, 0, 4, n0 + 1 - RING + 1)
                n = n0 + 2
                with sp.Fori(0, FSTEPS - 1) as i:
                    load_up(f, n, i + 1, 0, n - RING + 1 + 3 * i)
                    load_up(f, n + 1, i + 1, 4, n + 1 - RING + 1 + 3 * i)
                    load_down(f, n + 2, i, n + 2 - RING + 1 + 3 * i)
                n = n0 + 3 * FSTEPS - 1
                load_down(f, n, FSTEPS - 1, n - RING + 1)

            for t in range(NT):
                sp.dma_start(xs[:, t, :], x[0, t * P:(t + 1) * P, :]).then_inc(x_in[t], 16)
            for n in range(RING):
                load(n)
            sp.dma_start(cst[:, P:], consts[:, P:DECAY_AT]).then_inc(consts_in, 16)
            with nc.allow_non_contiguous_dma(reason="gains of a head: one element per partition"):
                for i, g in enumerate((ev_q_norm_g, ev_k_norm_g, q_norm_w_2, k_norm_w_2)):
                    for r in range(2):
                        sp.dma_start(head_gain[r * HD:(r + 1) * HD, i:i + 1],
                                     g[0].rearrange("(p o) -> p o", o=1)).then_inc(small_in, 16)
                sp.dma_start(pool_gain, ev_pool_scale[0].rearrange("(g p) -> p g", p=P)).then_inc(small_in, 16)
            sp.dma_start(poolw[:], ev_pool_w[0].rearrange("g c d -> c g d")).then_inc(small_in, 16)
            n = RING
            while n < N_UNITS:
                if n in U_FFN:
                    load_ffn(U_FFN.index(n))
                    n += 3 * FSTEPS
                else:
                    load(n)
                    n += 1
            for t in range(NT):
                for h in range(2):
                    sp.wait_ge(x_added, 4 * 5 + 2 * t + h + 1)
                    sp.dma_start(out[0, t * P:(t + 1) * P, h * 512:(h + 1) * 512], xs[:, t, h * 512:(h + 1) * 512]).then_inc(stored, 16)
            sp.wait_ge(stored, 16 * 2 * NT)

        @block.gpsimd
        def _(pool):
            def load_gain(k, m):
                pool.wait_ge(xn_ready, 4 * k_before[m])
                pool.dma_start(gains[:], NORM_G[k].partition_broadcast(P)).then_inc(gains_in, 16)

            k_before = {m: NORMS[m - 1] + 1 for m in range(1, len(NORMS))}
            nc.gpsimd.memset(neg_half, -0.5).then_inc(half_ready, 1)
            pool.wait_ge(half_ready, 1)

            def row_rstd(k, e):
                for t in range(NT):
                    i = 2 * k + t
                    pool.wait_ge(sumsq_ready, 2 * e + t + 1)
                    nc.gpsimd.tensor_scalar(msq[:, i:i + 1], sumsq[:, i:i + 1], 1.0 / D, EPS,
                                            ALU.mult, ALU.add).then_inc(msq_ready, 1)
                    pool.wait_ge(msq_ready, 2 * e + t + 1)
                    nc.gpsimd.tensor_tensor(rstd[:, i:i + 1], msq[:, i:i + 1], neg_half[:, 0:1],
                                            ALU.pow).then_inc(rstd_ready, 1)

            def head_rstd(events, n, k):
                for e in events:
                    pool.wait_ge(head_sum, e + 1)
                    nc.gpsimd.tensor_scalar(head_ms[:, e, 0:n], head_ss[:, e, 0:n], 1.0 / HD, EPS,
                                            ALU.mult, ALU.add).then_inc(head_ms_ready, 1)
                    pool.wait_ge(head_ms_ready, e + 1)
                    nc.gpsimd.tensor_tensor(head_rs[:, e, 0:n], head_ms[:, e, 0:n], neg_half[:, 0:n],
                                            ALU.pow).then_inc(head_pow_ready, 1)
                    pool.wait_ge(head_pow_ready, e + 1)
                    nc.gpsimd.tensor_scalar(head_rs[:, e, 0:n], head_rs[:, e, 0:n], x_rstd(k, e % 2), None,
                                            ALU.mult).then_inc(head_rs_ready, 1)

            row_rstd(0, 0)
            load_gain(1, 1)
            head_rstd((0, 1), 2, 0)
            head_rstd((2, 3), 8, 0)
            for e in (1, 2, 3, 4):
                row_rstd(e, e)
                if e == 1:
                    pool.wait_ge(pooled_ready, 1)
                    pool.dma_start(cst[:, CONST_COLS["bands"][0]:DECAY_AT], consts[:, DECAY_AT:]
                                   ).then_inc(decay_in, 16)
                load_gain(NORMS[e + 1], e + 1)
            head_rstd((4, 5, 6, 7), 8, 4)
            for t in range(NT):
                pool.wait_ge(gn_var_ready, t + 1)
                nc.gpsimd.tensor_scalar(gn_var[:, t, :], gn_mv[:, t, :, 1], 1.0, GN_EPS,
                                        ALU.mult, ALU.add).then_inc(gn_step, 1)
                pool.wait_ge(gn_step, t + 1)
                nc.gpsimd.tensor_tensor(gn_rstd[:, t, :], gn_var[:, t, :], neg_half[:, 0:RET_HEADS],
                                        ALU.pow).then_inc(gn_rstd_ready, 1)
            row_rstd(6, 5)

        @block.scalar
        def _(act):
            def split_high(n, i=0):
                if isinstance(i, int) and n + 3 * i >= N_UNITS:
                    return
                cols = sum(s.shape[0] // P * c for _, c, s in units[n]) if n < N_UNITS and units[n] else UNIT
                act.wait_ge(landed[n % RING], 32 * (n // RING + 1) + 32 * i)
                if n >= RING:
                    act.wait_ge(unit_used, n - RING + 1 + 3 * i)
                nc.scalar.activation(high[:, n % RING, 0:cols], raw[:, n % RING, 0:cols], ACT.Copy
                                     ).then_inc(high_ready, 1)

            def x_high(k, e, dst=xh, amid={}):
                for t in range(NT):
                    for q in range(2):
                        if (t, q) in amid:
                            split_high(amid[t, q])
                        act.wait_ge(xT_ready, 4 * k + 2 * t + q + 1)
                        nc.scalar.activation(dst[:, 4 * q:4 * q + 4, t * P:(t + 1) * P],
                                             bank(XT_BANKS[t][q]).rearrange("p (k n) -> p k n", k=4), ACT.Copy
                                             ).then_inc(xh_ready, 1)
                        if e is not None and q != t:
                            row_squares(k, e, t)

            def row_squares(k, e, t):
                if e:
                    act.wait_ge(x_added, 4 * (e - 1) + 2 * t + 2)
                else:
                    act.wait_ge(x_in[t], 16)
                if 2 * e + t:
                    act.wait_ge(sumsq_ready, 2 * e + t)
                nc.scalar.activation(junk, xs[:, t, :], ACT.Square, accum_out=sumsq[:, 2 * k + t:2 * k + t + 1]
                                     ).then_inc(sumsq_ready, 1)

            def head_squares(unit, events, n, k):
                for t, e in enumerate(events):
                    chunk_done(act, unit, t)
                    if e >= 2:
                        act.wait_ge(head_sum, e - 1)
                    sq = (e_sq if e < 4 else m_sq)[:, t, 0:n]
                    nc.scalar.activation(sq, bank(SETS[chunk_set(unit)][t], 0, n), ACT.Square,
                                         scale=x_rstd(k, t)).then_inc(head_sq, 1)

            def headT_copy(event, dst, src, gain):
                act.wait_ge(headT_ready, event)
                nc.scalar.activation(dst, src, ACT.Copy, scale=gain).then_inc(headT_copied, 1)

            def copy_chunk(unit, t, dst, done, k, func=ACT.Copy):
                chunk_done(act, unit, t)
                scale = x_rstd(k, t)
                nc.scalar.activation(dst, bank(SETS[chunk_set(unit)][t]), func, scale=scale).then_inc(done, 1)

            def softmax_exp(a, h, lb):
                act.wait_ge(max_ready, 2 * (8 * a + h) + 2)
                if h >= 2:
                    act.wait_ge(probsT_ready, 8 * a + h - 1)
                b = h % 2
                for t, (c0, c1) in enumerate(((0, P), (P, TRI))):
                    nc.scalar.activation(probs[:, b, c0:c1], bank(lb[b], c0, c1), ACT.Exp,
                                         bias=row_max[:, b, t:t + 1], accum_out=row_sum[:, b, t:t + 1]
                                         ).then_inc(exp_ready, 1)

            def softmax_T(a, h):
                act.wait_ge(probsT_ready, 8 * a + h + 1)
                if h >= 2:
                    act.wait_ge(pv_ready, 8 * a + h - 1)
                nc.scalar.activation(probsT[:, h % 2, :], bank(PT_BANK, 0, TRI), ACT.Copy).then_inc(probsT_copied, 1)

            def softmax_out(a, j):
                act.wait_ge(pv_ready, 8 * a + 2 * j + 2)
                nc.scalar.activation(mh[:, j, :], bank(PV_BANK, 0, SEQ), ACT.Copy).then_inc(pv_high, 1)

            def softmax_start(a, lb):
                softmax_exp(a, 0, lb)
                softmax_exp(a, 1, lb)

            def softmax_past(a, h):
                softmax_T(a, h)
                if h >= 2 and h % 2 == 0:
                    softmax_out(a, h // 2 - 1)

            def softmax_next(a, h, lb):
                if h + 2 < 8:
                    softmax_exp(a, h + 2, lb)

            def ffn(f):
                n0 = U_FFN[f]

                def gated(c):
                    for t in range(NT):
                        step_done(act, f, c, t)
                        if f or c_late(c):
                            act.wait_ge(hidden_ready, 2 * (FSTEPS * f + c) - 1 + t)
                        nc.scalar.activation(f_silu[:, t, :], bank(SETS[step_set(c)][t], 0, FC), ACT.Silu,
                                             scale=x_rstd(FFN_NORM[f], t)).then_inc(silu_ready, 1)

                def hiddenT(c):
                    act.wait_ge(hiddenT_ready, FSTEPS * f + c + 1)
                    if (f or c_late(c)) and not (isinstance(c, int) and c == FSTEPS - 1):
                        act.wait_ge(unit_used, n0 + 2 + 3 * c)
                    nc.scalar.activation(hidden_tile(gh, mh, c), bank(6).rearrange("p (k n) -> p k n", k=2), ACT.Copy).then_inc(gh_ready, 1)

                def step(c, i):
                    split_high(n0 + 4, i)
                    split_high(n0 + 5, i)
                    hiddenT(c - 1)
                    gated(c)
                    split_high(n0 + 6, i)

                split_high(n0 + 3)
                act.wait_ge(rstd_ready, 2 * NORMS.index(FFN_NORM[f]) + 2)
                gated(0)
                step(1, 0)
                with act.Fori(1, FSTEPS - 2) as i:
                    step(i + 1, i)
                step(FSTEPS - 1, FSTEPS - 2)
                hiddenT(FSTEPS - 1)
                split_high(n0 + 3 * FSTEPS + 1)

            act.dma_start(gains[:], NORM_G[0].partition_broadcast(P)).then_inc(first_gain_in, 16)
            act.dma_start(ident, consts[:, 0:P]).then_inc(ident_in, 16)
            x_high(0, None, amid={(1, 0): 0, (1, 1): 1})
            for t in range(NT):
                row_squares(0, 0, t)
            split_high(2)
            act.wait_ge(ident_in, 16)
            nc.scalar.activation(identr[:], ident, ACT.Copy).then_inc(masks_ready, 1)

            split_high(3)
            split_high(4)
            act.wait_ge(rstd_ready, 2)
            head_squares(U_KVQI, (0, 1), P, 0)
            for t in range(NT):
                nc.scalar.activation(e_vqi[:, t, :], bank(SET_A[t], P, 512), ACT.Copy, scale=x_rstd(0, t)).then_inc(vqi_copied, 1)
            for t in range(NT):
                chunk_done(act, U_KI, t)
                nc.scalar.activation(e_kk[:, t, :].rearrange("p (r d) -> p r d", r=2),
                                     bank(SET_C[t], 0, HD).unsqueeze(1).to_broadcast([P, 2, HD]), ACT.Copy, scale=x_rstd(0, t)
                                     ).then_inc(ki_copied, 1)
                nc.scalar.activation(idx_w[:, t, :], bank(SET_C[t], HD, KI_COLS), ACT.Copy, scale=x_rstd(0, t)
                                     ).then_inc(idx_w_copied, 1)
            split_high(5)
            split_high(6)
            act.wait_ge(small_in, 16 * 10)
            headT_copy(1, e_kT, bank(6, 0, SEQ), head_gain[:, 1:2])
            split_high(7)
            for t in range(NT):
                act.wait_ge(idx_ready, t + 1)
                k = (t + 1) * P
                nc.scalar.activation(e_rel[:, t, :, 0:k].rearrange("p (j b) k -> p b j k", b=2),
                                     psum[:, 4 + 2 * t:6 + 2 * t, 0:2 * k].rearrange("p b (j k) -> p b j k", j=2),
                                     ACT.Relu, scale=IDX_SCALE).then_inc(rel_ready, 1)
            for t in range(NT):
                copy_chunk(U_POOL, t, e_u[:, t, :], u_copied, 0)
            split_high(8)
            act.wait_ge(pooled_ready, 1)
            nc.scalar.activation(e_pm.rearrange("p (b j) n -> p b (j n)", b=2), psum[:, 4:6, :], ACT.Copy).then_inc(pooled_copied, 1)
            split_high(9)
            for g in range(4):
                act.wait_ge(poolmix_ready, 1)
                nc.scalar.activation(mh[:, 4 + g, :], bank(6 + g // 2, (g % 2) * SEQ, (g % 2 + 1) * SEQ), ACT.Copy,
                                     scale=pool_gain[:, g:g + 1]).then_inc(poolmix_high, 1)
            head_squares(U_Q, (2, 3), 512, 0)
            split_high(10)
            act.wait_ge(consts_in, 16)
            nc.scalar.activation(causalr[:], causal, ACT.Copy).then_inc(masks_ready, 1)
            nc.scalar.activation(strictr[:], const("strict"), ACT.Copy).then_inc(masks_ready, 1)
            split_high(U_EOUT + 3)
            act.wait_ge(q_gain_ready, 1)
            for t in range(NT):
                headT_copy(2 + t, e_qT[:, :, t * P:(t + 1) * P], bank(6 + t).rearrange("p (j n) -> p j n", j=4),
                           q_gain[:, 0:1])
            softmax_start(0, E_LB)
            for h in range(8):
                softmax_past(0, h)
                softmax_next(0, h, E_LB)
                if h == 5:
                    split_high(U_EOUT + 4)
            softmax_out(0, 3)
            split_high(U_EOUT + 5)
            x_high(1, 1)
            split_high(U_FFN[0] + 2)
            ffn(0)

            x_high(2, 2)
            split_high(U_QKV[0] + 2)
            act.wait_ge(rstd_ready, 6)

            def copy_T(half, f):
                for t in range(NT):
                    act.wait_ge(qkvT_ready, 4 * half + 2 * f + t + 1)
                    dst = (o_qT, o_kT)[f][:, half, :, t * P:(t + 1) * P]
                    nc.scalar.activation(dst, bank(QK_T_BANK[half, f] + t).rearrange("p (j n) -> p j n", j=4), ACT.Copy
                                         ).then_inc(qkvT_copied, 1)

            def stick_sigmoids(p):
                act.wait_ge(z_ready, p + 1)
                z = psum[:, Z_BANK:Z_BANK + 2, 0:TRI]
                if p:
                    act.wait_ge(later_ready, 4 * p)
                nc.scalar.activation(o_stay, z, ACT.Sigmoid, scale=-QK_SCALE).then_inc(stay_ready, 1)
                if p:
                    act.wait_ge(a_ready, p)
                nc.scalar.activation(o_beta, z, ACT.Sigmoid, scale=QK_SCALE).then_inc(beta_ready, 1)

            def stick_aT(p):
                act.wait_ge(aT_ready, p + 1)
                if p >= A_RING:
                    act.wait_ge(sbv_ready, p - A_RING + 1)
                nc.scalar.activation(o_aT[:, p % A_RING], psum[:, A_T_BANK:A_T_BANK + 2, 0:TRI], ACT.Copy).then_inc(aT_copied, 1)

            def stick_out(p):
                act.wait_ge(sbv_ready, p + 1)
                b = pv_bank(p)
                nc.scalar.activation(mh[:, p, :].rearrange("p (t n) -> p t n", t=NT), psum[:, b:b + 2, TRI:512], ACT.Copy
                                     ).then_inc(sbv_high, 1)

            for u in range(16):
                if u in A_T_BEFORE:
                    stick_aT(A_T_BEFORE[u])
                if u % 2 == 0 and 2 <= u <= 12:
                    c = u // 2 - 1
                    half, f = divmod(c, 2)
                    for t in range(NT):
                        if c < 4:
                            copy_chunk(U_QKV[c], t, o_tok[:, f, t, :], qkv_copied, 2)
                        else:
                            copy_chunk(U_QKV[c], t, o_v[:, c - 4, t, :], v_copied, 2)
                if u in QK_T_BEFORE:
                    copy_T(*QK_T_BEFORE[u])
                if u in Z_BEFORE:
                    stick_sigmoids(Z_BEFORE[u])
                if u:
                    split_high(U_QKV[0] + u + 2)
                if u in QK_T_MID:
                    copy_T(*QK_T_MID[u])
                for p in PV_MID.get(u, ()):
                    stick_out(p)
            x_high(3, 3)
            split_high(U_FFN[1] + 2)
            ffn(1)

            x_high(4, 4)
            split_high(U_P2[0] + 2)
            act.wait_ge(rstd_ready, 10)
            U = U_P2[0]
            for j in range(2 * len(U_P2)):
                c, last = divmod(j, 2)
                if 7 <= j < 15:
                    softmax_past(1, j - 7)
                if last:
                    unit = U_P2[c]
                    if c < 2:
                        head_squares(unit, (4 + 2 * c, 5 + 2 * c), 512, 4)
                    elif c == 2:
                        for t in range(NT):
                            copy_chunk(unit, t, m_v[:, t, :], mv_copied, 4)
                    elif c in (5, 6):
                        for t in range(NT):
                            copy_chunk(unit, t, r_v[:, t, (c - 5) * 512:(c - 4) * 512], rv_copied, 4)
                    elif c in (7, 8):
                        for t in range(NT):
                            copy_chunk(unit, t, r_gate[:, t, (c - 7) * 512:(c - 6) * 512], rg_ready, 4, ACT.Silu)
                    elif c >= 9:
                        g, half = divmod(c - 9, 2)
                        if half == 0 and g == 0:
                            act.wait_ge(logits_ready, 16)
                        if half == 0 and g == 1:
                            act.wait_ge(rscore_ready, RET_HEADS)
                        for t in range(NT):
                            copy_chunk(unit, t, (gate_a, gate_b)[g][:, t, half * 512:(half + 1) * 512], gates_ready, 4, ACT.Sigmoid)
                if j == 6:
                    softmax_start(1, M_LB)
                if 7 <= j < 15:
                    softmax_next(1, j - 7, M_LB)
                split_high(U + j + 3)
                if j == 3:
                    for t in range(NT):
                        headT_copy(4 + t, m_qT[:, :, t * P:(t + 1) * P], bank(4 + t).rearrange("p (j n) -> p j n", j=4),
                                   q_gain[:, 1:2])
                if j == 5:
                    for t in range(NT):
                        headT_copy(6 + t, m_kT[:, :, t * P:(t + 1) * P], bank(6 + t).rearrange("p (j n) -> p j n", j=4),
                                   head_gain[:, 3:4])
                if j == 15:
                    softmax_out(1, 3)
                if j in (16, 17):
                    for t in range(NT):
                        act.wait_ge(ropeT_ready, 2 * (j - 16) + t + 1)
                        nc.scalar.activation((r_qT, r_kT)[j - 16][:, :, t * P:(t + 1) * P],
                                             bank((4, 6)[j - 16] + t).rearrange("p (j n) -> p j n", j=4), ACT.Copy,
                                             scale=(1.0, RET_SCALE)[j - 16]).then_inc(ropeT_copied, 1)
            for t in range(NT):
                for q in range(2):
                    act.wait_ge(retT_ready, 2 * t + q + 1)
                    nc.scalar.activation(xh[:, 4 * q:4 * q + 4, t * P:(t + 1) * P],
                                         bank(2 + 2 * t + q).rearrange("p (k n) -> p k n", k=4), ACT.Copy).then_inc(ret_high, 1)
            split_high(U_MOBA + 3)
            split_high(U_MOBA + 4)
            for n in range(U_RET, U_WO - 1):
                split_high(n + 3)
            x_high(5, None, mh)
            for n in range(U_WO, U_FFN[2]):
                split_high(n + 2)
            x_high(6, 5)
            split_high(U_FFN[2] + 2)
            ffn(2)

        @block.vector
        def _(dve):
            def split_low(n, i=0):
                if isinstance(i, int) and n + 3 * i >= N_UNITS:
                    return
                cols = sum(s.shape[0] // P * c for _, c, s in units[n]) if n < N_UNITS and units[n] else UNIT
                dve.wait_ge(high_ready, n + 1 + 3 * i)
                nc.vector.tensor_tensor(low[:, n % RING, 0:cols], raw[:, n % RING, 0:cols],
                                        high[:, n % RING, 0:cols].bitcast(F32), ALU.subtract).then_inc(low_ready, 1)

            def half(h):
                return slice(h * 512, (h + 1) * 512)

            def x_low(k, t, q, hi=xh, lo=xl):
                dve.wait_ge(xh_ready, 4 * k + 2 * t + q + 1)
                s = (slice(None), slice(4 * q, 4 * q + 4), slice(t * P, (t + 1) * P))
                nc.vector.tensor_tensor(lo[s], bank(XT_BANKS[t][q]).rearrange("p (k n) -> p k n", k=4),
                                        hi[s].bitcast(F32), ALU.subtract).then_inc(xl_ready, 1)

            def x_parts(k, add, scale, hi=xh, lo=xl, amid={}):
                for h in range(2):
                    add(0, h)
                    scale(0, h)
                add(1, 0)
                scale(1, 0)
                x_low(k, 0, 0, hi, lo)
                add(1, 1)
                scale(1, 1)
                for t, q in ((0, 1), (1, 0), (1, 1)):
                    if (t, q) in amid:
                        split_low(amid[t, q])
                    x_low(k, t, q, hi, lo)

            def tall_done(unit, end, t):
                if t:
                    dve.wait_ge(unit_used, end)
                else:
                    dve.wait_ge(tall_first, TALLS[unit])

            def residual(unit, end, banks):
                def add(t, h):
                    tall_done(unit, end, t)
                    nc.vector.tensor_tensor(xs[:, t, half(h)], bank(banks[2 * t + h]), xs[:, t, half(h)], ALU.add
                                            ).then_inc(x_added, 1)
                return add

            def gained(k, e):
                def scale(t, h):
                    if e:
                        dve.wait_ge(x_added, 4 * (e - 1) + 2 * t + h + 1)
                        dve.wait_ge(gains_in, 16 * e)
                    else:
                        dve.wait_ge(x_in[t], 16)
                        dve.wait_ge(first_gain_in, 16)
                    nc.vector.tensor_tensor(xn[:, t, half(h)], xs[:, t, half(h)], gains[:, half(h)], ALU.mult
                                            ).then_inc(xn_ready, 1)
                return scale

            def head_sums(events, heads):
                for e in events:
                    dve.wait_ge(head_sq, e + 1)
                    sq = (e_sq if e < 4 else m_sq)[:, e % 2, 0:heads * HD]
                    nc.vector.tensor_reduce(head_ss[:, e, 0:heads], sq.rearrange("p (h d) -> p h d", h=heads),
                                            AX_X, ALU.add).then_inc(head_sum, 1)

            def head_scale(e, src, dst, heads):
                dve.wait_ge(head_rs_ready, e + 1)
                nc.vector.tensor_tensor(dst, src, heads, ALU.mult).then_inc(head_normed, 1)

            def softmax_max(a, h, lb):
                dve.wait_ge(logits_ready, 8 * a + h + 1)
                if h >= 2:
                    dve.wait_ge(exp_ready, 2 * (8 * a + h - 1))
                b = h % 2
                for t, (c0, c1) in enumerate(((0, P), (P, TRI))):
                    nc.vector.tensor_reduce(row_max[:, b, t:t + 1], bank(lb[b], c0, c1), AX_X, ALU.max, negate=True
                                            ).then_inc(max_ready, 1)

            def softmax_norm(a, h):
                b = h % 2
                dve.wait_ge(exp_ready, 2 * (8 * a + h) + 2)
                nc.vector.reciprocal(row_inv[:, b, :], row_sum[:, b, :]).then_inc(inv_ready, 1)
                dve.wait_ge(inv_ready, 8 * a + h + 1)
                for t, (c0, c1) in enumerate(((0, P), (P, TRI))):
                    nc.vector.tensor_scalar(probs[:, b, c0:c1], probs[:, b, c0:c1], row_inv[:, b, t:t + 1], None,
                                            ALU.mult).then_inc(probs_ready, 1)

            def softmax_out(a, j):
                dve.wait_ge(pv_high, 4 * a + j + 1)
                nc.vector.tensor_tensor(ml[:, j, :], bank(PV_BANK, 0, SEQ), mh[:, j, :].bitcast(F32), ALU.subtract
                                        ).then_inc(pv_low, 1)

            def softmax_start(a, lb):
                softmax_max(a, 0, lb)
                softmax_max(a, 1, lb)
                softmax_norm(a, 0)

            def softmax_head(a, h, lb):
                if h + 1 < 8:
                    softmax_norm(a, h + 1)
                if h >= 2 and h % 2 == 0:
                    softmax_out(a, h // 2 - 1)
                if h + 2 < 8:
                    softmax_max(a, h + 2, lb)

            def ffn(f):
                n0 = U_FFN[f]

                def gated(c):
                    for t in range(NT):
                        dve.wait_ge(silu_ready, 2 * (FSTEPS * f + c) + t + 1)
                        if f or c_late(c):
                            dve.wait_ge(hiddenT_ready, FSTEPS * f + c)
                        nc.vector.scalar_tensor_tensor(out=f_hidden[:, t, :], in0=bank(SETS[step_set(c)][t], FC, 2 * FC),
                                                       scalar=x_rstd(FFN_NORM[f], t), in1=f_silu[:, t, :],
                                                       op0=ALU.mult, op1=ALU.mult).then_inc(hidden_ready, 1)

                def hiddenT(c):
                    dve.wait_ge(gh_ready, FSTEPS * f + c + 1)
                    nc.vector.tensor_tensor(hidden_tile(gl, ml, c), bank(6).rearrange("p (k n) -> p k n", k=2),
                                            hidden_tile(gh, mh, c).bitcast(F32),
                                            ALU.subtract).then_inc(gl_ready, 1)

                def step(c, i):
                    split_low(n0 + 4, i)
                    split_low(n0 + 5, i)
                    hiddenT(c - 1)
                    gated(c)
                    if isinstance(c, int) and c == FSTEPS - 1:
                        hiddenT(c)
                    split_low(n0 + 6, i)

                split_low(n0 + 3)
                dve.wait_ge(rstd_ready, 2 * NORMS.index(FFN_NORM[f]) + 2)
                gated(0)
                step(1, 0)
                with dve.Fori(1, FSTEPS - 2) as i:
                    step(i + 1, i)
                step(FSTEPS - 1, FSTEPS - 2)
                return residual(n0, n0 + 3 * FSTEPS, TALL_MID)

            x_parts(0, lambda t, h: None, gained(0, 0), amid={(0, 1): 0, (1, 1): 1})
            split_low(2)

            split_low(3)
            head_sums((0, 1), 2)
            split_low(4)
            for t in range(NT):
                dve.wait_ge(vqi_copied, t + 1)
                head_scale(t, bank(SET_A[t], 0, P).rearrange("p (h d) -> p h d", h=2),
                           e_kn[:, t, :].rearrange("p (h d) -> p h d", h=2),
                           head_rs[:, t, 0:2].unsqueeze(2).to_broadcast([P, 2, HD]))
            split_low(5)
            dve.wait_ge(kiT_ready, 1)
            nc.vector.tensor_copy(e_kiT, bank(4, 0, SEQ)).then_inc(kiT_copied, 1)
            dve.wait_ge(qiT_ready, 1)
            nc.vector.tensor_copy(e_qiT, bank(5).rearrange("p (j n) -> p j n", j=2)).then_inc(qiT_copied, 1)
            split_low(6)
            dve.wait_ge(small_in, 16 * 10)
            nc.vector.tensor_scalar(q_gain, head_gain[:, 0:4:2], QK_SCALE, None, ALU.mult).then_inc(q_gain_ready, 1)
            split_low(7)
            steps = 0

            def step(ins):
                nonlocal steps
                steps += 1
                ins.then_inc(topk_step, 1)
                dve.wait_ge(topk_step, steps)

            dve.wait_ge(idx_w_copied, 2)
            dve.wait_ge(consts_in, 16)

            def topk(t):
                k = (t + 1) * P
                return slice(t * P, t * P + k), causal[:, t * P:t * P + k], e_score[:, 0:k]

            def topk_scores(t):
                cols, mask, score = topk(t)
                dve.wait_ge(rel_ready, t + 1)
                for h in range(IDX_HEADS):
                    step(nc.vector.scalar_tensor_tensor(out=score, in0=e_rel[:, t, h, 0:(t + 1) * P], scalar=idx_w[:, t, h:h + 1],
                                                        in1=score if h else mask, op0=ALU.mult, op1=ALU.add))

            def topk_rounds(t, rounds):
                cols, mask, score = topk(t)
                for _ in range(rounds):
                    step(nc.vector.max(top8, score))
                    step(nc.vector.match_replace(score, top8, score, TAKEN))

            def topk_mask(t):
                cols, mask, score = topk(t)
                hit = e_hit[:, 0:(t + 1) * P]
                step(nc.vector.tensor_scalar(hit, score, TAKEN, -MASKED, ALU.is_equal, ALU.mult))
                nc.vector.scalar_tensor_tensor(out=selbias[:, cols], in0=hit, scalar=MASKED, in1=mask, op0=ALU.add, op1=ALU.add
                                               ).then_inc(sel_ready, 1)

            ROUNDS, EARLY_ROUNDS = N_SEL // 8, 4
            topk_scores(0)
            topk_rounds(0, ROUNDS)
            topk_mask(0)
            split_low(8)
            topk_scores(1)
            topk_rounds(1, EARLY_ROUNDS)
            for g in range(4):
                dve.wait_ge(poolmix_high, 2 * (g // 2) + 2)
                nc.vector.scalar_tensor_tensor(out=ml[:, 4 + g, :], in0=bank(6 + g // 2, (g % 2) * SEQ, (g % 2 + 1) * SEQ),
                                               scalar=pool_gain[:, g:g + 1], in1=mh[:, 4 + g, :].bitcast(F32),
                                               op0=ALU.mult, op1=ALU.subtract).then_inc(poolmix_low, 1)
            head_sums((2, 3), 8)
            split_low(9)
            for t in range(NT):
                head_scale(2 + t, bank(SET_A[t]).rearrange("p (g r d) -> p g r d", g=2, r=4),
                           e_qn[:, t, :].rearrange("p (r g d) -> p g r d", g=2, r=4),
                           head_rs[:, 2 + t, :].rearrange("p (g r) -> p g r", g=2).unsqueeze(3).to_broadcast([P, 2, 4, HD]))
            topk_rounds(1, ROUNDS - EARLY_ROUNDS)
            topk_mask(1)
            softmax_start(0, E_LB)
            for h in range(8):
                softmax_head(0, h, E_LB)
                if h == 4:
                    split_low(U_EOUT + 2)
            split_low(U_EOUT + 3)
            softmax_out(0, 3)
            split_low(U_EOUT + 4)
            x_parts(1, residual(U_EOUT, U_FFN[0], TALL_MID), gained(1, 1), amid={(1, 1): U_EOUT + 5})
            split_low(U_FFN[0] + 2)
            add = ffn(0)

            x_parts(2, add, gained(2, 2), amid={(1, 1): U_QKV[0] + 1})
            split_low(U_QKV[0] + 2)

            def stick_weights(p):
                dve.wait_ge(stay_ready, p + 1)
                if p:
                    dve.wait_ge(a_ready, p)
                else:
                    dve.wait_ge(ones_set, 1)
                for e in range(2):
                    for c0, c1 in ((0, P), (P, TRI)):
                        stay = o_stay[:, e, c0 + 1:c1][:, ::-1]
                        nc.vector.tensor_tensor_scan(o_later[:, e, c0:c1 - 1][:, ::-1], stay, stay, 1.0,
                                                     ALU.mult, ALU.min).then_inc(later_ready, 1)
                dve.wait_ge(later_ready, 4 * p + 4)
                dve.wait_ge(beta_ready, p + 1)
                if p:
                    dve.wait_ge(aT_ready, p)
                nc.vector.tensor_tensor(o_a, o_beta, o_later, ALU.mult).then_inc(a_ready, 1)

            def stick_out(p):
                dve.wait_ge(sbv_high, p + 1)
                b = pv_bank(p)
                nc.vector.tensor_tensor(ml[:, p, :].rearrange("p (t n) -> p t n", t=NT), psum[:, b:b + 2, TRI:512],
                                        mh[:, p, :].bitcast(F32).rearrange("p (t n) -> p t n", t=NT), ALU.subtract
                                        ).then_inc(sbv_low, 1)

            nc.vector.memset(o_later.rearrange("p e (b n) -> p e b n", n=P)[:, :, 0:TRI // P:2, P - 1], 1.0).then_inc(ones_set, 1)
            for u in range(16):
                if u in Z_BEFORE:
                    stick_weights(Z_BEFORE[u])
                for p in PV_MID.get(u, ()):
                    stick_out(p)
                if 0 < u < 15:
                    split_low(U_QKV[0] + u + 2)
            x_parts(3, residual(U_OOUT, U_FFN[1], TALL_LOW), gained(3, 3), amid={(1, 1): U_FFN[1] + 1})
            split_low(U_FFN[1] + 2)
            add = ffn(1)

            x_parts(4, add, gained(4, 4), amid={(1, 1): U_P2[0] + 1})
            split_low(U_P2[0] + 2)
            dve.wait_ge(rstd_ready, 10)
            gn_steps = 0
            U = U_P2[0]
            for j in range(2 * len(U_P2)):
                c, last = divmod(j, 2)
                if last and c < 2:
                    head_sums((4 + 2 * c, 5 + 2 * c), 8)
                if j == 6:
                    softmax_start(1, M_LB)
                if 7 <= j < 15:
                    softmax_head(1, j - 7, M_LB)
                if last and c in (3, 4):
                    unit = U_P2[c]
                    s = chunk_set(unit)
                    for t in range(NT):
                        chunk_done(dve, unit, t)
                        src = bank(SETS[s][t]).rearrange("p (h x d) -> p h x d", h=RET_HEADS, x=2)
                        dst = r_tok[:, t, c - 3, :].rearrange("p (h x d) -> p h x d", h=RET_HEADS, x=2)
                        tmp = r_half[:, t, :].rearrange("p (h x d) -> p h x d", h=RET_HEADS, x=2)
                        table = rope[:, t].rearrange("p c (x d) -> p c x d", x=2)

                        def spread(r, x):
                            return table[:, r, x, :].unsqueeze(1).to_broadcast([P, RET_HEADS, HD])

                        for x in range(2):
                            nc.vector.scalar_tensor_tensor(out=dst[:, :, x, :], in0=src[:, :, x, :], scalar=x_rstd(4, t), in1=spread(0, x),
                                                           op0=ALU.mult, op1=ALU.mult).then_inc(rope_step, 1)
                            nc.vector.scalar_tensor_tensor(out=tmp[:, :, x, :], in0=src[:, :, 1 - x, :], scalar=x_rstd(4, t), in1=spread(1, x),
                                                           op0=ALU.mult, op1=ALU.mult).then_inc(rope_step, 1)
                        dve.wait_ge(rope_step, 4 * (2 * (c - 3) + t + 1))
                        nc.vector.tensor_tensor(r_tok[:, t, c - 3, :], r_tok[:, t, c - 3, :], r_half[:, t, :], ALU.add).then_inc(roped, 1)
                if j == 15:
                    softmax_out(1, 3)
                split_low(U + j + 3)
                if last and c < 2:
                    for t in range(NT):
                        if c == 1:
                            dve.wait_ge(headT_ready, 4 + t + 1 - 1)
                        head_scale(4 + 2 * c + t, bank(SETS[c][t]).rearrange("p (h d) -> p h d", h=8),
                                   m_tok[:, t, :].rearrange("p (h d) -> p h d", h=8),
                                   head_rs[:, 4 + 2 * c + t, :].unsqueeze(2).to_broadcast([P, 8, HD]))
                if j == 18:
                    dve.wait_ge(decay_in, 16)
                    for h in range(RET_HEADS):
                        dve.wait_ge(rscore_ready, h + 1)
                        nc.vector.tensor_tensor(r_a[:, h, :], bank(4 + h, 0, TRI), decay[:, h, :], ALU.mult).then_inc(decayed, 1)
                if j == 20:
                    for t in range(NT):
                        for h in range(RET_HEADS):
                            dve.wait_ge(ro_ready, h + 1)
                            nc.vector.bn_stats(gn_stats[:, t, h, :], bank(4 + h, t * RET_DV, (t + 1) * RET_DV)).then_inc(gn_done, 1)
                        for h in range(RET_HEADS):
                            dve.wait_ge(gn_done, RET_HEADS * t + h + 1)
                            ins = nc.vector.bn_aggr(gn_mv[:, t, h, :], gn_stats[:, t, h, :])
                        ins.then_inc(gn_var_ready, 1)
                if j == 22:
                    dve.wait_ge(rg_ready, 4)
                    for t in range(NT):
                        dve.wait_ge(gn_rstd_ready, t + 1)
                        for h in range(RET_HEADS):
                            s = slice(h * RET_DV, (h + 1) * RET_DV)
                            nc.vector.tensor_scalar(r_o[:, t, s], bank(4 + h, t * RET_DV, (t + 1) * RET_DV),
                                                    gn_mv[:, t, h, 0:1], gn_rstd[:, t, h:h + 1], ALU.subtract, ALU.mult
                                                    ).then_inc(ret_ready, 1)
                        dve.wait_ge(ret_ready, 5 * t + RET_HEADS)
                        nc.vector.tensor_tensor(r_o[:, t, :], r_o[:, t, :], r_gate[:, t, :], ALU.mult).then_inc(ret_ready, 1)
            for t in range(NT):
                for q in range(2):
                    dve.wait_ge(ret_high, 2 * t + q + 1)
                    s = (slice(None), slice(4 * q, 4 * q + 4), slice(t * P, (t + 1) * P))
                    nc.vector.tensor_tensor(xl[s], bank(2 + 2 * t + q).rearrange("p (k n) -> p k n", k=4),
                                            xh[s].bitcast(F32), ALU.subtract).then_inc(ret_low, 1)

            split_low(U_MOBA + 3)
            split_low(U_MOBA + 4)
            dve.wait_ge(gates_ready, 8)
            for t in range(NT):
                tall_done(U_MOBA, U_RET, t)
                for h in range(2):
                    nc.vector.tensor_tensor(gate_b[:, t, half(h)], bank(TALL_ENDS[2 * t + h]), gate_b[:, t, half(h)], ALU.mult
                                            ).then_inc(b_gated, 1)
            for n in range(U_RET, U_WO - 2):
                split_low(n + 3)

            def gate(t, h):
                tall_done(U_RET, U_WO, t)
                nc.vector.tensor_tensor(gate_a[:, t, half(h)], bank(TALL_MID[2 * t + h]), gate_a[:, t, half(h)], ALU.mult
                                        ).then_inc(a_gated, 1)

            def mix(t, h):
                dve.wait_ge(a_gated, 2 * t + h + 1)
                dve.wait_ge(b_gated, 2 * t + h + 1)
                dve.wait_ge(retT_ready, 4)
                nc.vector.tensor_tensor(xn[:, t, half(h)], gate_a[:, t, half(h)], gate_b[:, t, half(h)], ALU.add
                                        ).then_inc(xn_ready, 1)

            x_parts(5, gate, mix, mh, ml, amid={(1, 1): U_WO + 1})
            for n in range(U_WO, U_FFN[2] - 1):
                split_low(n + 2)
            x_parts(6, residual(U_WO, U_FFN[2], TALL_SPLIT), gained(6, 5), amid={(1, 1): U_FFN[2] + 1})
            split_low(U_FFN[2] + 2)
            add = ffn(2)
            for t in range(NT):
                for h in range(2):
                    add(t, h)

        @block.tensor
        def _(pe):
            def three_products(out, n, k, cols, sh, sl, c0, c1, start, stop):
                wh, wl = slot_tile(high, n, k, cols)[:, c0:c1], slot_tile(low, n, k, cols)[:, c0:c1]
                nc.tensor.matmul(out, sh, wh, start=start, stop=False, skip_group_check=True)
                nc.tensor.matmul(out, sh, wl, start=False, stop=False, skip_group_check=True)
                return nc.tensor.matmul(out, sl, wh, start=False, stop=stop, skip_group_check=True)

            def wait_x(k, t, q):
                pe.wait_ge(xl_ready, 4 * k + 2 * t + q + 1)

            def wide_unit(n, second, banks, cols, done, i=0, xk=None, mid=None):
                pe.wait_ge(low_ready, n + 1 + 3 * i)
                for t in range(NT):
                    if xk is not None:
                        wait_x(xk, t, second)
                    for k in range(4):
                        kk = 4 * second + k
                        s = (slice(None), kk, slice(t * P, (t + 1) * P))
                        ins = three_products(bank(banks[t], 0, cols), n, k, cols, xh[s], xl[s], 0, cols,
                                             kk == 0, kk == KD - 1)
                    if second and t == 0:
                        ins.then_inc(done, 1)
                    if mid and t == 0:
                        mid()
                ins.then_inc(unit_used, 1)

            def wide(unit, second, cols=512, xk=None, mid=None):
                s = chunk_set(unit)
                if not second:
                    for q, v in reads_before(unit):
                        pe.wait_ge(q, v)
                wide_unit(unit + second, second, SETS[s], cols, wide_ready[s], xk=xk, mid=mid)

            def tall_unit(n, sh, sl, k0, banks, start, stop, i=0, mid=None, xk=None):
                pe.wait_ge(low_ready, n + 1 + 3 * i)
                for t in range(NT):
                    if xk is not None:
                        wait_x(xk, t, k0 // 4)
                    for k in range(2):
                        s = (slice(None), k0 + k, slice(t * P, (t + 1) * P))
                        for h in range(2):
                            ins = three_products(bank(banks[2 * t + h]), n, k, D, sh[s], sl[s], h * 512, (h + 1) * 512,
                                                 start and k == 0, stop and k == 1)
                    if stop and t == 0:
                        ins.then_inc(tall_first, 1)
                    if mid and t == 0:
                        mid()
                ins.then_inc(unit_used, 1)

            def transposes(dst_bank, srcs, done):
                for j, src in enumerate(srcs):
                    ins = nc.tensor.transpose(bank(dst_bank, j * P, (j + 1) * P), src, ident)
                ins.then_inc(done, 1)

            def xT(k, parts):
                for t, q in parts:
                    pe.wait_ge(xn_ready, 4 * k + 2 * t + q + 1)
                    transposes(XT_BANKS[t][q], [xn[:, t, (4 * q + j) * P:(4 * q + j + 1) * P] for j in range(4)], xT_ready)

            XT_BEFORE, XT_MID = ((0, 0), (0, 1), (1, 0)), ((1, 1),)

            def softmax_logits(a, h, lb, qT, kT, mask):
                b = h % 2
                if h >= 2:
                    pe.wait_ge(exp_ready, 2 * (8 * a + h - 1))
                for t, (c0, c1) in enumerate(((0, P), (P, TRI))):
                    dst = bank(lb[b], c0, c1)
                    nc.tensor.matmul(dst, qT[:, t * P:(t + 1) * P], kT[:, 0:c1 - c0], start=True, stop=False, skip_group_check=True)
                    ins = nc.tensor.matmul(dst, identr[:], mask[:, c0:c1], start=False, stop=True, skip_group_check=True)
                ins.then_inc(logits_ready, 1)

            def softmax_T(a, h):
                pe.wait_ge(probs_ready, 2 * (8 * a + h) + 2)
                if h:
                    pe.wait_ge(probsT_copied, 8 * a + h)
                b = h % 2
                transposes(PT_BANK, [probs[:, b, j * P:(j + 1) * P] for j in range(3)], probsT_ready)

            def softmax_pv(a, h, v):
                b = h % 2
                pe.wait_ge(probsT_copied, 8 * a + h + 1)
                if h >= 2:
                    pe.wait_ge(pv_low, 4 * a + h // 2)
                rows = slice(b * HD, (b + 1) * HD)
                dst = [psum[rows, PV_BANK, t * P:(t + 1) * P] for t in range(NT)]
                nc.tensor.matmul(dst[0], v(0), probsT[:, b, 0:P], start=True, stop=True, skip_group_check=True)
                nc.tensor.matmul(dst[1], v(0), probsT[:, b, P:2 * P], start=True, stop=False, skip_group_check=True)
                nc.tensor.matmul(dst[1], v(1), probsT[:, b, 2 * P:TRI], start=False, stop=True, skip_group_check=True
                                 ).then_inc(pv_ready, 1)

            def ffn(f, xk):
                n0 = U_FFN[f]

                def hiddenT(c):
                    pe.wait_ge(hidden_ready, 2 * (FSTEPS * f + c) + 2)
                    if f or c_late(c):
                        pe.wait_ge(gl_ready, FSTEPS * f + c)
                    transposes(6, [f_hidden[:, t, k * P:(k + 1) * P] for k in range(2) for t in range(NT)], hiddenT_ready)

                def down(n, c, start, stop, i=0, mid=None):
                    pe.wait_ge(gl_ready, FSTEPS * f + c + 1)
                    tall_unit(n, hidden_tile(gh, mh, c), hidden_tile(gl, ml, c), 0, TALL_MID, start, stop, i, mid)

                def step(c, i, start, mid=None):
                    n = n0 + 2
                    if not (isinstance(c, int) and c == 1):
                        pe.wait_ge(hidden_ready, 2 * (FSTEPS * f + c))
                    wide_unit(n, 0, SET_A, 512, wide_ready[0], i)
                    hiddenT(c - 1)
                    wide_unit(n + 1, 1, SET_A, 512, wide_ready[0], i)
                    down(n + 2, c - 1, start, False, i, mid)

                xT(xk, XT_BEFORE)
                wide_unit(n0, 0, SET_C, 512, wide_ready[2], xk=xk, mid=lambda: xT(xk, XT_MID))
                wide_unit(n0 + 1, 1, SET_C, 512, wide_ready[2], xk=xk)
                step(1, 0, True)
                with pe.Fori(1, FSTEPS - 2) as i:
                    step(i + 1, i, False)
                step(FSTEPS - 1, FSTEPS - 2, False, mid=lambda: hiddenT(FSTEPS - 1))
                down(n0 + 3 * FSTEPS - 1, FSTEPS - 1, False, True)

            pe.wait_ge(ident_in, 16)
            xT(0, XT_BEFORE)
            wide(U_KVQI, 0, xk=0, mid=lambda: xT(0, XT_MID))
            wide(U_KVQI, 1, xk=0)
            wide(U_KI, 0, KI_COLS)
            wide(U_KI, 1, KI_COLS)

            def index_T():
                pe.wait_ge(ki_copied, 2)
                pe.wait_ge(idx_w_copied, 2)
                transposes(4, [e_kk[:, t, :] for t in range(NT)], kiT_ready)
                pe.wait_ge(vqi_copied, 2)
                transposes(5, [e_vqi[:, t, P + j * P:P + (j + 1) * P] for j in range(2) for t in range(NT)], qiT_ready)

            def index_scores():
                pe.wait_ge(kiT_copied, 1)
                pe.wait_ge(qiT_copied, 1)
                pe.wait_ge(headT_copied, 1)
                for t in range(NT):
                    k = (t + 1) * P
                    for h in range(IDX_HEADS):
                        rows = slice((h % 2) * HD, (h % 2 + 1) * HD)
                        ins = nc.tensor.matmul(bank(4 + 2 * t + h % 2, (h // 2) * k, (h // 2 + 1) * k),
                                               e_qiT[rows, h // 2, t * P:(t + 1) * P], e_kiT[rows, 0:k], start=True, stop=True,
                                               skip_group_check=True)
                    ins.then_inc(idx_ready, 1)

            def pooling():
                pe.wait_ge(u_copied, 2)
                pe.wait_ge(rel_ready, 1)
                pe.wait_ge(consts_in, 16)
                for g in range(4):
                    dst = bank(4 + g // 2, (g % 2) * SEQ, (g % 2 + 1) * SEQ)
                    c = slice(g * P, (g + 1) * P)
                    nc.tensor.matmul(dst, e_u[:, 0, c], bands[:, g, 0:SEQ], start=True, stop=False, skip_group_check=True)
                    ins = nc.tensor.matmul(dst[:, P:SEQ], e_u[:, 1, c], bands[:, g, SEQ:TRI], start=False, stop=True,
                                           skip_group_check=True)
                ins.then_inc(pooled_ready, 1)

            def pool_mix():
                pe.wait_ge(pooled_copied, 1)
                pe.wait_ge(rel_ready, 2)
                pe.wait_ge(small_in, 16 * 10)
                for g in range(4):
                    ins = nc.tensor.matmul(bank(6 + g // 2, (g % 2) * SEQ, (g % 2 + 1) * SEQ), poolw[:, g, :], e_pm[:, g, :],
                                           start=True, stop=True, skip_group_check=True)
                ins.then_inc(poolmix_ready, 1)

            def even_qT():
                for t in range(NT):
                    pe.wait_ge(head_normed, 3 + t)
                    transposes(6 + t, [e_qn[:, t, j * P:(j + 1) * P] for j in range(4)], headT_ready)

            wide(U_POOL, 0, mid=index_T)
            pe.wait_ge(head_normed, 2)
            transposes(6, [e_kn[:, t, :] for t in range(NT)], headT_ready)
            wide(U_POOL, 1, mid=index_scores)
            wide(U_Q, 0, mid=pooling)
            wide(U_Q, 1, mid=pool_mix)

            def even_logits(h):
                g, r = divmod(h, 4)
                rows = slice(g * HD, (g + 1) * HD)
                softmax_logits(0, h, E_LB, e_qT[rows, r, :], e_kT[rows, :], selbias)

            def first_logits():
                pe.wait_ge(masks_ready, 1)
                pe.wait_ge(headT_copied, 3)
                pe.wait_ge(sel_ready, 2)
                even_logits(0)
                even_logits(1)

            pe.wait_ge(poolmix_low, 4)
            tall_unit(U_EOUT, mh, ml, 4, TALL_MID, True, False)
            even_qT()
            tall_unit(U_EOUT + 1, mh, ml, 6, TALL_MID, False, False, mid=first_logits)

            def even_pv(h):
                softmax_pv(0, h, lambda b: e_vqi[:, b, (h // 4) * HD:(h // 4 + 1) * HD])

            for h in range(7):
                if h + 2 < 8:
                    even_logits(h + 2)
                softmax_T(0, h)
                if h:
                    even_pv(h - 1)

            def last_head():
                softmax_T(0, 7)
                even_pv(6)
                even_pv(7)

            pe.wait_ge(pv_low, 2)
            tall_unit(U_EOUT + 2, mh, ml, 0, TALL_MID, False, False, mid=last_head)
            pe.wait_ge(pv_low, 4)
            tall_unit(U_EOUT + 3, mh, ml, 2, TALL_MID, False, True)
            ffn(0, 1)

            xT(2, XT_BEFORE)

            def qk_T(half, f):
                for t in range(NT):
                    pe.wait_ge(qkv_copied, 4 * half + 2 * f + t + 1)
                    transposes(QK_T_BANK[half, f] + t, [o_tok[:, f, t, j * P:(j + 1) * P] for j in range(4)], qkvT_ready)

            def stick_z(p):
                half, j = divmod(p, 4)
                if j == 0:
                    pe.wait_ge(qkvT_copied, 4 * half + 4)
                    pe.wait_ge(masks_ready, 3)
                if p:
                    pe.wait_ge(beta_ready, p)
                done = sum(len(ps) for u, ps in PV_MID.items() if u < 6 + p)
                if done:
                    pe.wait_ge(sbv_low, done)
                for e in range(2):
                    rows = slice(e * HD, (e + 1) * HD)
                    q, k = o_qT[rows, half, j, :], o_kT[rows, half, j, :]
                    for t, (c0, c1) in enumerate(((0, P), (P, TRI))):
                        nc.tensor.matmul(bank(Z_BANK + e, c0, c1), q[:, t * P:(t + 1) * P], k[:, 0:c1 - c0], start=True, stop=False,
                                         skip_group_check=True)
                        ins = nc.tensor.matmul(bank(Z_BANK + e, c1 - P, c1), identr[:], strictr[:], start=False, stop=True,
                                               skip_group_check=True)
                ins.then_inc(z_ready, 1)

            def stick_aT(p):
                pe.wait_ge(a_ready, p + 1)
                if p == 0:
                    pe.wait_ge(qkvT_copied, 4)
                if p == 1:
                    pe.wait_ge(qkvT_copied, 6)
                if p == 3:
                    pe.wait_ge(qkvT_copied, 8)
                if p:
                    pe.wait_ge(aT_copied, p)
                done = sum(len(ps) for u, ps in PV_MID.items() if u < 7 + p)
                if done:
                    pe.wait_ge(sbv_low, done)
                for e in range(2):
                    for j in range(3):
                        ins = nc.tensor.transpose(bank(A_T_BANK + e, j * P, (j + 1) * P), o_a[:, e, j * P:(j + 1) * P], ident)
                ins.then_inc(aT_ready, 1)

            def stick_pv(p, u):
                half, j = divmod(p, 4)
                pe.wait_ge(aT_copied, A_T_BEFORE.get(u, 0) + 1 if pv_bank(p) == A_T_BANK else p + 1)
                if pv_bank(p) == Z_BANK:
                    pe.wait_ge(beta_ready, min(Z_BEFORE.get(u, 7), 7) + 1)
                pe.wait_ge(v_copied, 2 * half + 2)
                for e in range(2):
                    a = o_aT[:, p % A_RING, e, :]
                    v = [o_v[:, half, b, (2 * j + e) * HD:(2 * j + e + 1) * HD] for b in range(NT)]
                    dst = [psum[e * HD:(e + 1) * HD, pv_bank(p) + t, TRI:512] for t in range(NT)]
                    nc.tensor.matmul(dst[0], v[0], a[:, 0:P], start=True, stop=True, skip_group_check=True)
                    nc.tensor.matmul(dst[1], v[0], a[:, P:SEQ], start=True, stop=False, skip_group_check=True)
                    ins = nc.tensor.matmul(dst[1], v[1], a[:, SEQ:TRI], start=False, stop=True, skip_group_check=True)
                ins.then_inc(sbv_ready, 1)

            for u in range(16):
                if u in QK_T_BEFORE:
                    qk_T(*QK_T_BEFORE[u])
                if u in A_T_BEFORE:
                    stick_aT(A_T_BEFORE[u])
                if u in Z_BEFORE:
                    stick_z(Z_BEFORE[u])

                def mid():
                    if u == 0:
                        xT(2, XT_MID)
                    if u in QK_T_MID:
                        pe.wait_ge(aT_copied, A_T_BEFORE[u] + 1)
                        qk_T(*QK_T_MID[u])
                    if u == 12:
                        pe.wait_ge(v_copied, 4)
                    for p in PV_MID.get(u, ()):
                        stick_pv(p, u)

                if u < 12:
                    wide(U_QKV[u // 2], u % 2, xk=2 if u < 2 else None, mid=mid)
                else:
                    p = u - 12
                    if p == 0:
                        pe.wait_ge(v_copied, 2)
                    pe.wait_ge(sbv_low, 2 * p + 2)
                    tall_unit(U_OOUT + p, mh, ml, 2 * p, TALL_LOW, p == 0, p == 3, mid=mid)
            ffn(1, 3)

            xT(4, XT_BEFORE)

            def moba_logits(h):
                rows = slice((h % 2) * HD, (h % 2 + 1) * HD)
                softmax_logits(1, h, M_LB, m_qT[rows, h // 2, :], m_kT[rows, h // 2, :], causalr)

            for j in range(2 * len(U_P2)):
                c, second = divmod(j, 2)

                def mid():
                    if j == 0:
                        xT(4, XT_MID)
                    if 8 <= j < 16:
                        h = j - 8
                        softmax_pv(1, h, lambda b: m_v[:, b, h * HD:(h + 1) * HD])

                wide(U_P2[c], second, xk=4 if j < 2 else None, mid=mid)
                if j in (3, 5):
                    f = (j - 3) // 2
                    for t in range(NT):
                        pe.wait_ge(head_normed, 4 + 2 * f + t + 1)
                        transposes(4 + 2 * f + t, [m_tok[:, t, i * P:(i + 1) * P] for i in range(4)], headT_ready)
                if j == 6:
                    pe.wait_ge(headT_copied, 7)
                    moba_logits(0)
                    moba_logits(1)
                    pe.wait_ge(mv_copied, 2)
                if 7 <= j < 15:
                    h = j - 7
                    softmax_T(1, h)
                    if h + 2 < 8:
                        moba_logits(h + 2)
                if j in (16, 17):
                    f = j - 16
                    pe.wait_ge(pv_low, 8)
                    for t in range(NT):
                        pe.wait_ge(roped, 2 * f + t + 1)
                        transposes(4 + 2 * f + t, [r_tok[:, t, f, i * P:(i + 1) * P] for i in range(4)], ropeT_ready)
                if j == 18:
                    pe.wait_ge(ropeT_copied, 4)
                    for h in range(RET_HEADS):
                        nc.tensor.matmul(bank(4 + h, 0, SEQ), r_kT[:, h, 0:P], r_qT[:, h, :], start=True, stop=True, skip_group_check=True)
                        nc.tensor.matmul(bank(4 + h, SEQ, TRI), r_kT[:, h, P:SEQ], r_qT[:, h, P:SEQ], start=True, stop=True,
                                         skip_group_check=True).then_inc(rscore_ready, 1)
                if j == 20:
                    pe.wait_ge(rv_copied, 4)
                    for h in range(RET_HEADS):
                        pe.wait_ge(decayed, h + 1)
                        v = [r_v[:, b, h * RET_DV:(h + 1) * RET_DV] for b in range(NT)]
                        nc.tensor.matmul(bank(4 + h, 0, RET_DV), r_a[:, h, 0:P], v[0], start=True, stop=True, skip_group_check=True)
                        nc.tensor.matmul(bank(4 + h, RET_DV, 512), r_a[:, h, P:SEQ], v[0], start=True, stop=False, skip_group_check=True)
                        nc.tensor.matmul(bank(4 + h, RET_DV, 512), r_a[:, h, SEQ:TRI], v[1], start=False, stop=True,
                                         skip_group_check=True).then_inc(ro_ready, 1)
            pe.wait_ge(gates_ready, 8)
            pe.wait_ge(ret_ready, 5 * NT)
            for t in range(NT):
                for q in range(2):
                    transposes(2 + 2 * t + q, [r_o[:, t, (4 * q + i) * P:(4 * q + i + 1) * P] for i in range(4)], retT_ready)
            for p in range(2):
                tall_unit(U_MOBA + p, mh, ml, 2 * p, TALL_ENDS, p == 0, p == 1)
            pe.wait_ge(ret_low, 4)
            for p in range(4):
                tall_unit(U_RET + p, xh, xl, 2 * p, TALL_MID, p == 0, p == 3)
            pe.wait_ge(b_gated, 4)
            xT(5, XT_BEFORE)
            for p in range(4):
                tall_unit(U_WO + p, mh, ml, 2 * p, TALL_SPLIT, p == 0, p == 3, mid=(lambda: xT(5, XT_MID)) if p == 0 else None, xk=5)
            ffn(2, 6)


_INS = ['x', 'norm_mix_g', 'norm_ffn_g', 'ev_w_in', 'ev_w_out', 'ev_q_norm_g', 'ev_k_norm_g', 'ev_pool_w',
        'ev_pool_scale', 'od_w_qkv', 'od_w_out', 'ffn_w1', 'ffn_w3', 'ffn_w2', 'norm1_w_2', 'w_in_2', 'q_norm_w_2',
        'k_norm_w_2', 'w_ret_out_2', 'w_moba_out_2', 'w_o_2', 'norm2_w_2', 'w_ffn_gate_2', 'w_ffn_up_2',
        'w_ffn_down_2']


def kernel(**inputs):
    import concourse.bacc as bacc
    from concourse.bass_utils import run_bass_kernel_spmd

    nc = bacc.Bacc("TRN2", target_bir_lowering=False, num_devices=1)
    arrays, args = {}, []
    for name in _INS:
        a = np.ascontiguousarray(inputs[name])
        arrays[f"in_{name}"] = a
        args.append(nc.dram_tensor(f"in_{name}", a.shape, mybir.dt.from_np(a.dtype), kind="ExternalInput").ap())
    arrays["consts"] = constants()
    args.append(nc.dram_tensor("consts", (P, CONST_N), F32, kind="ExternalInput").ap())
    args.append(nc.dram_tensor("out", (1, SEQ, D), F32, kind="ExternalOutput").ap())
    program(nc, *args)
    r = run_bass_kernel_spmd(nc, [arrays], core_ids=[0])
    return r.results[0]["out"]
```
